# Optimizing a Trainium2 kernel written in Bass

```python
import math
import jax, jax.numpy as jnp
from jax import lax
import numpy as np

D_MODEL = 2048
BATCH = 1
SEQ = 256
DEPTH = 1

MIX_WIDTH = D_MODEL
HGRN_WIDTH = MIX_WIDTH // 2
HGRN_DK = 128
HGRN_HEADS = HGRN_WIDTH // HGRN_DK
HGRN_DV = HGRN_WIDTH // HGRN_HEADS
FOURIER_WIDTH = MIX_WIDTH - HGRN_WIDTH
FOURIER_GROUPS = 4
FOURIER_GDIM = FOURIER_WIDTH // FOURIER_GROUPS
CHUNK = 64
D_FF = int(math.ceil((8 * D_MODEL / 3) / 256) * 256)
PROJ_WIDTH = 5 * HGRN_WIDTH + FOURIER_WIDTH
DEEPNORM_ALPHA = (2.0 * DEPTH) ** 0.25
DEEPNORM_BETA = (8.0 * DEPTH) ** -0.25
LN_EPS = 1e-5
RMS_EPS = 1e-6

kernel_name = "hgrn2_fourier_hybrid_deepnorm_encoder"

def _layernorm(x, g, b):
    xf = x.astype(jnp.float32)
    mu = jnp.mean(xf, axis=-1, keepdims=True)
    var = jnp.mean(jnp.square(xf - mu), axis=-1, keepdims=True)
    y = (xf - mu) * lax.rsqrt(var + LN_EPS) * g.astype(jnp.float32) + b.astype(jnp.float32)
    return y.astype(x.dtype)

def _chunk_recurrence(q, k, v, logf):
    B, T, H, K = q.shape
    V = v.shape[-1]
    N = T // CHUNK
    qc = q.reshape(B, N, CHUNK, H, K)
    kc = k.reshape(B, N, CHUNK, H, K)
    vc = v.reshape(B, N, CHUNK, H, V)
    bcum = jnp.cumsum(logf.reshape(B, N, CHUNK, H, K), axis=2)
    b_last = bcum[:, :, -1:]
    q_dec = qc * jnp.exp(bcum)
    k_inv = kc * jnp.exp(-bcum)
    k_end = kc * jnp.exp(b_last - bcum)
    scores = jnp.einsum('bnthk,bnshk->bnhts', q_dec, k_inv)
    tri = jnp.tril(jnp.ones((CHUNK, CHUNK), dtype=bool))
    scores = jnp.where(tri, scores, 0.0)
    o_intra = jnp.einsum('bnhts,bnshv->bnthv', scores, vc)
    d_state = jnp.einsum('bnshk,bnshv->bnhkv', k_end, vc)
    decay = jnp.exp(b_last[:, :, 0])

    def step(S, inp):
        d, ds = inp
        return d[..., None] * S + ds, S

    S0 = jnp.zeros((B, H, K, V), dtype=q.dtype)
    _, S_prev = lax.scan(step, S0, (jnp.moveaxis(decay, 1, 0), jnp.moveaxis(d_state, 1, 0)))
    S_prev = jnp.moveaxis(S_prev, 0, 1)
    o_inter = jnp.einsum('bnthk,bnhkv->bnthv', q_dec, S_prev)
    return (o_intra + o_inter).reshape(B, T, H, V)

def _forget(z, lb):
    f = lb + (1.0 - lb) * jax.nn.sigmoid(z.astype(jnp.float32))
    return jnp.log(f), 1.0 - f

def _hgrn2_group(q_raw, i_raw, zf, zb, g_raw, lb_f, lb_b, g_norm):
    B, T, _ = q_raw.shape
    shp_k = (B, T, HGRN_HEADS, HGRN_DK)
    shp_v = (B, T, HGRN_HEADS, HGRN_DV)
    q = jax.nn.silu(q_raw.astype(jnp.float32)).reshape(shp_k)
    v = i_raw.astype(jnp.float32).reshape(shp_v)
    logf_f, k_f = _forget(zf, lb_f)
    logf_b, k_b = _forget(zb, lb_b)
    o_fwd = _chunk_recurrence(q, k_f.reshape(shp_k), v, logf_f.reshape(shp_k))
    flip = lambda a: jnp.flip(a, axis=1)
    o_bwd = flip(_chunk_recurrence(flip(q), flip(k_b.reshape(shp_k)), flip(v), flip(logf_b.reshape(shp_k))))
    o = o_fwd + o_bwd
    o = o * lax.rsqrt(jnp.mean(jnp.square(o), axis=-1, keepdims=True) + RMS_EPS) * g_norm.astype(jnp.float32)
    o = o * jax.nn.silu(g_raw.astype(jnp.float32)).reshape(shp_v)
    return o.reshape(B, T, HGRN_WIDTH).astype(q_raw.dtype)

def _fourier_group(u):
    B, T, _ = u.shape
    ug = u.astype(jnp.float32).reshape(B, T, FOURIER_GROUPS, FOURIER_GDIM)
    y = jnp.real(jnp.fft.fft2(ug, axes=(1, 3), norm='ortho'))
    return y.reshape(B, T, FOURIER_WIDTH).astype(u.dtype)

def setup_inputs(seed: int = 0) -> dict:
    key = jax.random.key(seed)
    ks = jax.random.split(key, 16)
    f32 = jnp.float32
    x = jax.random.normal(ks[0], (BATCH, SEQ, D_MODEL), f32)
    ln_emb_g = 1.0 + 0.02 * jax.random.normal(ks[1], (D_MODEL,), f32)
    ln_emb_b = 0.02 * jax.random.normal(ks[2], (D_MODEL,), f32)
    w_in = jax.random.normal(ks[3], (DEPTH, D_MODEL, PROJ_WIDTH), f32) * D_MODEL ** -0.5
    lb_fwd_logits = 0.5 * jax.random.normal(ks[4], (DEPTH + 1, HGRN_WIDTH), f32)
    lb_bwd_logits = 0.5 * jax.random.normal(ks[5], (DEPTH + 1, HGRN_WIDTH), f32)
    g_norm = 1.0 + 0.02 * jax.random.normal(ks[6], (DEPTH, HGRN_DV), f32)
    w_out = jax.random.normal(ks[7], (DEPTH, MIX_WIDTH, D_MODEL), f32) * (MIX_WIDTH ** -0.5 * DEEPNORM_BETA)
    ln1_g = 1.0 + 0.02 * jax.random.normal(ks[8], (DEPTH, D_MODEL), f32)
    ln1_b = 0.02 * jax.random.normal(ks[9], (DEPTH, D_MODEL), f32)
    w_gate = jax.random.normal(ks[10], (DEPTH, D_MODEL, D_FF), f32) * D_MODEL ** -0.5
    w_up = jax.random.normal(ks[11], (DEPTH, D_MODEL, D_FF), f32) * D_MODEL ** -0.5
    w_down = jax.random.normal(ks[12], (DEPTH, D_FF, D_MODEL), f32) * (D_FF ** -0.5 * DEEPNORM_BETA)
    ln2_g = 1.0 + 0.02 * jax.random.normal(ks[13], (DEPTH, D_MODEL), f32)
    ln2_b = 0.02 * jax.random.normal(ks[14], (DEPTH, D_MODEL), f32)
    return {"x": x, "ln_emb_g": ln_emb_g, "ln_emb_b": ln_emb_b, "w_in": w_in,
            "lb_fwd_logits": lb_fwd_logits, "lb_bwd_logits": lb_bwd_logits, "g_norm": g_norm,
            "w_out": w_out, "ln1_g": ln1_g, "ln1_b": ln1_b, "w_gate": w_gate, "w_up": w_up,
            "w_down": w_down, "ln2_g": ln2_g, "ln2_b": ln2_b}

def reference(x, ln_emb_g, ln_emb_b, w_in, lb_fwd_logits, lb_bwd_logits, g_norm,
              w_out, ln1_g, ln1_b, w_gate, w_up, w_down, ln2_g, ln2_b):
    lb_fwd_all = jnp.cumsum(jax.nn.softmax(lb_fwd_logits.astype(jnp.float32), axis=0), axis=0)
    lb_bwd_all = jnp.cumsum(jax.nn.softmax(lb_bwd_logits.astype(jnp.float32), axis=0), axis=0)
    h = _layernorm(x, ln_emb_g, ln_emb_b)
    W = HGRN_WIDTH
    for l in range(DEPTH):
        u = h @ w_in[l]
        q_raw = u[..., 0 * W:1 * W]
        i_raw = u[..., 1 * W:2 * W]
        zf = u[..., 2 * W:3 * W]
        zb = u[..., 3 * W:4 * W]
        g_raw = u[..., 4 * W:5 * W]
        u_four = u[..., 5 * W:5 * W + FOURIER_WIDTH]
        o_hgrn = _hgrn2_group(q_raw, i_raw, zf, zb, g_raw, lb_fwd_all[l], lb_bwd_all[l], g_norm[l])
        o_four = _fourier_group(u_four)
        mix = jnp.concatenate([o_hgrn, o_four], axis=-1) @ w_out[l]
        h = _layernorm(DEEPNORM_ALPHA * h + mix, ln1_g[l], ln1_b[l])
        ffn = (jax.nn.silu(h @ w_gate[l]) * (h @ w_up[l])) @ w_down[l]
        h = _layernorm(DEEPNORM_ALPHA * h + ffn, ln2_g[l], ln2_b[l])
    return h


_drawn_inputs = setup_inputs


def setup_inputs(seed=0):
    import zlib

    import numpy as np

    out = dict(_drawn_inputs(seed))
    spreads = {}
    factors = {'lb_fwd_logits': 8.0,
     'lb_bwd_logits': 8.0,
     'g_norm': 8.0,
     'ln1_g': 2.746,
     'ln1_b': 2.669,
     'ln2_g': 2.774,
     'ln2_b': 2.788}
    for name, (base, spread) in spreads.items():
        noise = np.random.default_rng([zlib.crc32(name.encode()), seed]).standard_normal(out[name].shape)
        drawn = base * np.exp(spread * noise) if base else spread * noise
        out[name] = __import__('jax').numpy.asarray(drawn.astype(out[name].dtype))
    for name, factor in factors.items():
        out[name] = (out[name] * factor).astype(out[name].dtype)
    return out
```

```python
import math
from contextlib import ExitStack

import concourse.bass as bass
from concourse import mybir

F32 = mybir.dt.float32
F32R = mybir.dt.float32r
U32 = mybir.dt.uint32
ALU = mybir.AluOpType
ACT = mybir.ActivationFunctionType

P = 128
T = 256
TT = T // P
D = 2048
KC = D // P
NB = 512
HEADS = 8
CH = 64
NCH = T // CH
FF = int(math.ceil((8 * D / 3) / 256) * 256)
FC = FF // P
GLU = FF // NB
RING = 4
SLOTS = KC // 2
DOWN_SLOTS = FC // 2
OUT0 = 12
GLU0 = 16
DOWN0 = GLU0 + 2 * GLU
DOWN_N0 = DOWN0 * SLOTS
ALPHA = 2.0 ** 0.25
LN_EPS = 1e-5
RMS_EPS = 1e-6
MIX_ORDER = [8, 10, 12, 0, 2, 14, 4, 6]
STATS = 6
VEC_ROWS = 96
SBUF_START = 16 * 1024 + 512
SBUF_END = 224 * 1024


def build(nc, A):
    with ExitStack() as ctx:
        place = {"at": SBUF_START}

        def sb(name, shape, dt=F32, at=None):
            size = 4 * math.prod(shape[1:])
            if at is None:
                at = place["at"]
                place["at"] += (size + 31) // 32 * 32
            return nc.alloc_sbuf_tensor_at(name, shape, dt, offset=at)

        def sem(name):
            return ctx.enter_context(nc.semaphore(name))

        rows = sb("rows", [P, TT, D])
        xT_hi = sb("xT_hi", [P, KC, T], F32R)
        xT_lo = sb("xT_lo", [P, KC, T], F32R)
        raw = [sb(f"raw{i}", [P, 2, NB]) for i in range(RING)]
        w_hi = [sb(f"w_hi{i}", [P, 2, NB], F32R) for i in range(RING)]
        w_lo = [sb(f"w_lo{i}", [P, 2, NB], F32R) for i in range(RING)]
        vecT = sb("vecT", [P, VEC_ROWS])
        mean_var = sb("mean_var", [P, TT, 2])
        stats = sb("stats", [P, TT, 4, STATS])
        var_eps = sb("var_eps", [P, TT])
        rstd = sb("rstd", [P, TT])
        minus_half = sb("minus_half", [P, TT])
        ident = sb("ident", [P, P])
        region = place["at"]
        mix_hi = sb("mix_hi", [P, KC, T], F32R)
        mix_lo = sb("mix_lo", [P, KC, T], F32R)
        consts = sb("consts", [P, 4 * T])
        tok_z = sb("tok_z", [P, TT, NB])
        tok_q = sb("tok_q", [P, TT, 2 * P])
        v = [sb(f"v{i}", [P, TT, 2 * P]) for i in range(2)]
        f = [sb(f"f{i}", [P, 2, 2, T + 2]) for i in range(2)]
        qT = [sb(f"qT{i}", [P, 2, T]) for i in range(2)]
        o_heads_at = place["at"]
        o_heads = sb("o_heads", [P, TT, HEADS * P])
        turned = [sb(f"turned{i}", [P, 2, T], at=place["at"] + 8 * T * i) for i in range(2)]
        k_end = sb("k_end", [P, 2, T])
        q_inv = sb("q_inv", [P, 2, T])
        q_dec = [sb(f"q_dec{i}", [P, 2, T]) for i in range(2)]
        heads_in = sb("heads_in", [P, 2, T])
        k_rows = sb("k_rows", [P, 2, TT, P])
        scoresT = sb("scoresT", [P, 2, TT, P])
        scores_sum = sb("scores_sum", [P, TT, P])
        state = sb("state", [P, 2, 3, P])
        squares = sb("squares", [P, P])
        g_norm = sb("g_norm", [P, P])
        decay = [sb(f"decay{i}", [P, 2, NCH]) for i in range(2)]
        inv_decay = sb("inv_decay", [P, 2, NCH])
        ssq = sb("ssq", [P, TT])
        rms_in = sb("rms_in", [P, TT])
        rms = sb("rms", [P, TT])
        lb_max = sb("lb_max", [P, 2, HEADS])
        lb_exp = sb("lb_exp", [P, 2, 2, HEADS])
        lb_sum = sb("lb_sum", [P, 2, HEADS])
        lb = sb("lb", [P, 2, HEADS])
        one_minus_lb = sb("one_minus_lb", [P, 2, HEADS])
        dft_hi = sb("dft_hi", [P, TT, 2 * T], F32R)
        dft_lo = sb("dft_lo", [P, TT, 2 * T], F32R)
        four = place["at"]
        u_hi = sb("u_hi", [P, TT, NB], F32R)
        u_lo = sb("u_lo", [P, TT, NB], F32R)
        dftT_hi = sb("dftT_hi", [P, 2, 2 * T], F32R)
        dftT_lo = sb("dftT_lo", [P, 2, 2 * T], F32R)
        dft_raw = sb("dft_raw", [P, TT, 2 * T], at=o_heads_at)
        vec_rows = sb("vec_rows", [VEC_ROWS, P], at=o_heads_at + 4 * TT * 2 * T)
        place["at"] = region
        act_hi = sb("act_hi", [P, FC, T], F32R)
        act_lo = sb("act_lo", [P, FC, T], F32R)
        silu = sb("silu", [P, TT, NB])
        gb_at = max(place["at"], four)
        gamma = sb("gamma", [P, D], at=gb_at)
        beta = sb("beta", [P, D], at=gb_at + 4 * D)

        assert max(place["at"], gb_at + 8 * D) <= SBUF_END, (place["at"], gb_at + 8 * D)

        first_ones = consts[:, 0:T]
        last_ones = consts[:, T:2 * T]
        causal = consts[:, 2 * T:4 * T].bitcast(U32).rearrange("p (d m t) -> p d m t", d=2, m=TT)

        acc = [ctx.enter_context(nc.psum_tensor(f"acc{i}", [P, TT, NB], F32)) for i in range(2)]
        bank = ctx.enter_context(nc.psum_tensor("bank", [P, 4, NB], F32))

        def dstate(d, c):
            at = {(0, 0): 0, (0, 2): 1, (1, 2): 2, (0, 1): 0, (1, 1): 1, (1, 3): 2}[d, c]
            return bank[:, 3 - c % 2, at * P:(at + 1) * P]

        x_landed = [sem(f"x_landed{i}") for i in range(4)]
        vec_landed = sem("vec_landed")
        ident_landed = sem("ident_landed")
        consts_landed = sem("consts_landed")
        gb_landed = sem("gb_landed")
        slot_landed = [sem(f"slot_landed{i}") for i in range(RING)]
        hi_ready = sem("hi_ready")
        lo_ready = sem("lo_ready")
        slots_done = sem("slots_done")
        acc_read = [sem("acc_read0"), sem("acc_read1")]
        vec_turned = sem("vec_turned")
        vec_ready = sem("vec_ready")
        lb_shifted = sem("lb_shifted")
        lb_exped = sem("lb_exped")
        lb_ready = sem("lb_ready")
        dft_hi_ready = sem("dft_hi_ready")
        pool_step = sem("pool_step")
        var_ready = sem("var_ready")
        rstd_ready = sem("rstd_ready")
        normed = sem("normed")
        rows_turned = sem("rows_turned")
        xT_hi_ready = sem("xT_hi_ready")
        turned_ready = sem("turned_ready")
        xT_lo_ready = sem("xT_lo_ready")
        z_turned = sem("z_turned")
        f_ready = sem("f_ready")
        qv_read = sem("qv_read")
        q_turned = sem("q_turned")
        qT_ready = sem("qT_ready")
        head_ready = sem("head_ready")
        k_turned = sem("k_turned")
        scores_done = sem("scores_done")
        k_rows_ready = sem("k_rows_ready")
        scores_ready = sem("scores_ready")
        dstate_done = sem("dstate_done")
        states_ready = sem("states_ready")
        out_done = sem("out_done")
        ssq_ready = sem("ssq_ready")
        rms_ready = sem("rms_ready")
        o_ready = sem("o_ready")
        sig_ready = sem("sig_ready")
        gated = sem("gated")
        gated_turned = sem("gated_turned")
        u_hi_ready = sem("u_hi_ready")
        four1_done = sem("four1_done")
        dftT_hi_ready = sem("dftT_hi_ready")
        dftT_ready = sem("dftT_ready")
        four2_done = sem("four2_done")
        mix_hi_ready = sem("mix_hi_ready")
        mix_ready = sem("mix_ready")
        residual_done = sem("residual_done")
        dft_ready = sem("dft_ready")
        act_turned = sem("act_turned")
        act_hi_ready = sem("act_hi_ready")
        act_ready = sem("act_ready")
        dve_step = sem("dve_step")
        out_ready = sem("out_ready")
        out_landed = sem("out_landed")

        x_rows = A["x"][0].rearrange("(m p) d -> p m d", p=P)
        out_rows = A["out"][0].rearrange("(m p) d -> m p d", p=P)
        w_in = A["w_in"][0]
        win_pairs = w_in.rearrange("(s c p) (m z n) -> s m p c z n", c=2, p=P, z=2, n=1024)
        win_cols = w_in.rearrange("(s c p) n -> s p c n", c=2, p=P)
        wout_cols = A["w_out"][0].rearrange("(s c p) n -> s p c n", c=2, p=P)
        wgate_cols = A["w_gate"][0].rearrange("(s c p) n -> s p c n", c=2, p=P)
        wup_cols = A["w_up"][0].rearrange("(s c p) n -> s p c n", c=2, p=P)
        wdown_cols = A["w_down"][0].rearrange("(s c p) n -> s p c n", c=2, p=P)

        block = ctx.enter_context(nc.Block())

        @block.sync
        def _(sp):
            for q in range(4):
                sp.dma_start(rows[:, :, q * NB:(q + 1) * NB],
                             x_rows[:, :, q * NB:(q + 1) * NB]).then_inc(x_landed[q], 16)

            def load_pair(head_pair, n0, first):
                for which in range(2):
                    for s in range(SLOTS):
                        n = which * SLOTS + s
                        r = s % RING
                        dst = raw[r][:, :, :].rearrange("p c (z n) -> p c z n", z=2)
                        for c in range(2):
                            src = win_pairs[s, 1 - which, :, c, :, bass.ds(head_pair, 2 * P)]
                            if c == 0 and not (first and n < RING):
                                sp.wait_ge(lo_ready, n0 + (n - RING + 1))
                            sp.dma_start(dst[:, c], src).then_inc(slot_landed[r], 16)

            def load(src, dst_slot, freed):
                sp.wait_ge(lo_ready, freed)
                sp.dma_start(raw[dst_slot][:, :, :], src).then_inc(slot_landed[dst_slot], 16)

            load_pair(0, 0, True)
            with sp.Fori(2, 5) as i:
                load_pair(i * (2 * P) - 2 * P, i * (2 * SLOTS) - 2 * SLOTS, False)
            for b in range(8, OUT0):
                col = 5 * 1024 + (b - 8) * NB if b < 10 else 4 * 1024 + (b - 10) * NB
                for s in range(SLOTS):
                    load(win_cols[s, :, :, col:col + NB], s % RING, b * SLOTS + s - RING + 1)
            with sp.Fori(1, D // NB + 1) as i:
                col = i * NB - NB
                for s in range(SLOTS):
                    load(wout_cols[MIX_ORDER[s] // 2, :, :, bass.ds(col, NB)], s % RING,
                         i * SLOTS + ((OUT0 - 1) * SLOTS + s - RING + 1))
            with sp.Fori(0, GLU) as i:
                col = sp.snap(i * NB)
                for which, cols in enumerate((wgate_cols, wup_cols)):
                    for s in range(SLOTS):
                        load(cols[s, :, :, bass.ds(col, NB)], s % RING,
                             i * (2 * SLOTS) + ((GLU0 + which) * SLOTS + s - RING + 1))
            with sp.Fori(0, D // NB // 2) as i:
                col = sp.snap(i * (2 * NB))
                for half in range(2):
                    for s in range(DOWN_SLOTS):
                        n = half * DOWN_SLOTS + s
                        load(wdown_cols[s, :, :, bass.ds(col + half * NB, NB)], n % RING,
                             i * (2 * DOWN_SLOTS) + (DOWN_N0 + n - RING + 1))
            for q in range(4):
                for m in range(TT):
                    sp.wait_ge(out_ready, q * TT + m + 1)
                    sp.dma_start(out_rows[m][:, q * NB:(q + 1) * NB],
                                 rows[:, m, q * NB:(q + 1) * NB]).then_inc(out_landed, 16)
            sp.wait_ge(out_landed, 16 * 4 * TT)

        @block.gpsimd
        def _(pool):
            steps = [0]

            def then(ins):
                steps[0] += 1
                ins.then_inc(pool_step, 1)
                pool.wait_ge(pool_step, steps[0])

            then(pool.memset(minus_half[:, :], -0.5))

            def layer_norm_rstd(i):
                pool.wait_ge(var_ready, i + 1)
                then(pool.tensor_scalar(var_eps[:, :], mean_var[:, :, 1], 1.0, LN_EPS, ALU.mult, ALU.add))
                pool.tensor_tensor(rstd[:, :], var_eps[:, :], minus_half[:, :], ALU.pow).then_inc(rstd_ready, 1)

            def xT_lows(i):
                for s in range(1, SLOTS):
                    pool.wait_ge(turned_ready, SLOTS * i + s + 1)
                    pool.tensor_tensor(xT_lo[:, 2 * s:2 * s + 2, :], turned[s % 2][:, :, :],
                                       xT_hi[:, 2 * s:2 * s + 2, :], ALU.subtract).then_inc(xT_lo_ready, 1)

            layer_norm_rstd(0)
            xT_lows(0)
            for h in range(HEADS):
                pool.wait_ge(ssq_ready, 2 * (h + 1))
                then(pool.tensor_scalar(rms_in[:, :], ssq[:, :], 1.0 / P, RMS_EPS, ALU.mult, ALU.add))
                pool.tensor_tensor(rms[:, :], rms_in[:, :], minus_half[:, :], ALU.pow).then_inc(rms_ready, 1)
            layer_norm_rstd(1)
            xT_lows(1)
            layer_norm_rstd(2)

        @block.scalar
        def _(act):
            vec_src = [A["ln_emb_g"], A["ln_emb_b"], A["ln1_g"][0], A["ln1_b"][0]]
            for i, a in enumerate(vec_src):
                act.dma_start(vec_rows[i * KC:(i + 1) * KC, :],
                              a.rearrange("(k p) -> k p", p=P)).then_inc(vec_landed, 16)
            for i, a in enumerate((A["lb_fwd_logits"], A["lb_bwd_logits"])):
                act.dma_start(vec_rows[4 * KC + 16 * i:4 * KC + 16 * (i + 1), :],
                              a.rearrange("l (h p) -> (l h) p", p=P)).then_inc(vec_landed, 16)
            act.dma_start(ident[:, :], A["consts"][:, 0:P]).then_inc(ident_landed, 16)

            def load_gamma_beta(g, b):
                for dst, src in ((gamma, g), (beta, b)):
                    act.dma_start(dst[:, :], src.rearrange("(a d) -> a d", a=1).broadcast_to([P, D]))\
                       .then_inc(gb_landed, 16)

            def load_constants():
                act.dma_start(consts[:, :], A["consts"][:, P:]).then_inc(consts_landed, 16)
                act.dma_start(dft_raw[:, :, :], A["dft"].rearrange("(m p) n -> p m n", p=P))\
                   .then_inc(consts_landed, 16)
                act.dma_start(g_norm[:, :], A["g_norm"].broadcast_to([P, P])).then_inc(consts_landed, 16)

            def split_hi(n, r, landed, used=None):
                act.wait_ge(slot_landed[r], landed)
                if used is not None:
                    act.wait_ge(slots_done, used)
                act.activation(w_hi[r][:, :, :], raw[r][:, :, :], ACT.Copy).then_inc(hi_ready, 1)

            def split(n):
                r, turn = n % RING, n // RING
                landed = 32 * (turn + 1) if n < 64 else 32 * 16 + 16 * (turn - 15)
                split_hi(n, r, landed, n - RING + 1 if n >= RING else None)

            def norm_pair(i, s):
                act.wait_ge(rows_turned, SLOTS * i + s + 1)
                for c in range(2):
                    k = 2 * s + c
                    col = 2 * KC * i + k
                    ins = act.activation(xT_hi[:, k, :], bank[:, s % 4, c * T:(c + 1) * T], ACT.Identity,
                                         bias=vecT[:, col + KC:col + KC + 1], scale=vecT[:, col:col + 1])
                ins.then_inc(xT_hi_ready, 1)

            split(0)
            split(1)
            act.wait_ge(vec_ready, 1)
            norm_pair(0, 0)
            norm_pair(0, 1)
            load_gamma_beta(A["ln_emb_g"], A["ln_emb_b"])
            for s in range(2, SLOTS):
                norm_pair(0, s)
                split(s)
                if s == 2:
                    load_constants()
            for b in range(1, OUT0 + 1):
                for s in range(SLOTS):
                    split(b * SLOTS + s)
                    if (b, s) == (1, 0):
                        act.wait_ge(lb_shifted, 1)
                        act.activation(lb_exp[:, :, :, :], lb_exp[:, :, :, :], ACT.Exp).then_inc(lb_exped, 1)
                    if (b, s) == (2, 0):
                        act.wait_ge(consts_landed, 48)
                        act.activation(dft_hi[:, :, :], dft_raw[:, :, :], ACT.Copy).then_inc(dft_hi_ready, 1)
                    if b < 9 and b % 2 == 1 and s == 3:
                        p = b // 2
                        act.wait_ge(slots_done, b * SLOTS)
                        if p:
                            act.wait_ge(z_turned, p)
                        act.activation(tok_z[:, :, :], acc[0][:, :, :], ACT.Sigmoid).then_inc(acc_read[0], 1)
                    if b < 9 and b % 2 == 1 and s in (6, 7):
                        p, d = b // 2, s - 6
                        act.wait_ge(z_turned, p + 1)
                        if p >= 2:
                            act.wait_ge(head_ready, 2 * p - 2)
                        if p == 0:
                            act.wait_ge(lb_ready, 1)
                        for e in range(2):
                            h = 2 * p + e
                            ins = act.activation(f[p % 2][:, d, e, 1:T + 1], bank[:, d, e * T:(e + 1) * T],
                                                 ACT.Identity, bias=lb[:, d, h:h + 1],
                                                 scale=one_minus_lb[:, d, h:h + 1])
                            ins.then_inc(f_ready, 1)
                    if 2 <= b < 10 and b % 2 == 0 and s == 3:
                        p = b // 2 - 1
                        act.wait_ge(slots_done, b * SLOTS)
                        if p:
                            act.wait_ge(q_turned, p)
                        act.activation(tok_q[:, :, :], acc[1][:, :, 0:2 * P], ACT.Sigmoid).then_inc(qv_read, 1)
                        if p >= 2:
                            act.wait_ge(out_done, 2 * p - 2)
                        act.activation(v[p % 2][:, :, :], acc[1][:, :, 2 * P:4 * P], ACT.Copy).then_inc(qv_read, 1)
                    if 3 <= b < 3 + HEADS and s == 6:
                        h = b - 3
                        act.wait_ge(k_turned, h + 1)
                        if h:
                            act.wait_ge(dstate_done, h)
                        act.activation(k_rows[:, :, :, :].rearrange("p d m k -> p (d m k)"),
                                       bank[:, 3, :], ACT.Copy).then_inc(k_rows_ready, 1)
                    if 4 <= b < 4 + HEADS and s == 4:
                        h = b - 4
                        act.wait_ge(out_done, h + 1)
                        if h:
                            act.wait_ge(rms_ready, h)
                        for m in range(TT):
                            if h or m:
                                act.wait_ge(ssq_ready, 2 * h + m)
                            act.activation(squares[:, :], bank[:, 3, m * P:(m + 1) * P], ACT.Square,
                                           accum_out=ssq[:, m:m + 1]).then_inc(ssq_ready, 1)
                    if (b, s) in ((9, 3), (10, 6)):
                        i = b - 9
                        act.wait_ge(slots_done, b * SLOTS)
                        if i:
                            act.wait_ge(four1_done, 2)
                        act.activation(u_hi[:, :, :], acc[i][:, :, :], ACT.Copy).then_inc(u_hi_ready, 1)
                    if (b, s) in ((9, 7), (10, 6), (11, 5), (12, 3)):
                        g = b - 9
                        act.wait_ge(four1_done, g + 1)
                        if g:
                            act.wait_ge(four2_done, g)
                        act.activation(dftT_hi[:, :, 0:T], bank[:, 0:2, 0:T], ACT.Copy).then_inc(dftT_hi_ready, 1)
                        act.activation(dftT_hi[:, :, T:2 * T], bank[:, 0:2, T:2 * T], ACT.Copy,
                                       scale=-1.0).then_inc(dftT_hi_ready, 1)
                    if (b, s) in ((10, 3), (11, 1), (12, 0), (12, 5)):
                        g = ((10, 3), (11, 1), (12, 0), (12, 5)).index((b, s))
                        act.wait_ge(four2_done, g + 1)
                        act.activation(mix_hi[:, 8 + 2 * g:10 + 2 * g, :].rearrange("p c t -> p (c t)"),
                                       bank[:, 0, :], ACT.Copy).then_inc(mix_hi_ready, 1)
                    if (b, s) in ((11, 3), (12, 2)):
                        i = b - 11
                        act.wait_ge(slots_done, b * SLOTS)
                        if i:
                            act.wait_ge(gated_turned, 1)
                        else:
                            act.wait_ge(z_turned, 4)
                        act.activation(tok_z[:, :, :], acc[i][:, :, :], ACT.Sigmoid).then_inc(sig_ready, 1)
                    if (b, s) in ((12, 1), (12, 6)):
                        i = (0, 1)[s == 6]
                        act.wait_ge(gated_turned, i + 1)
                        for c in range(2):
                            k = 4 * i + 2 * c
                            act.activation(mix_hi[:, k:k + 2, :].rearrange("p c t -> p (c t)"),
                                           bank[:, 2 + c, :], ACT.Copy).then_inc(mix_hi_ready, 1)
            act.wait_ge(four2_done, 4)
            load_gamma_beta(A["ln1_g"][0], A["ln1_b"][0])
            for n in range((OUT0 + 1) * SLOTS, GLU0 * SLOTS):
                split(n)
            for n in range(GLU0 * SLOTS, (GLU0 + 2) * SLOTS):
                split(n)
                s = n - GLU0 * SLOTS
                if s == 3:
                    for pair in range(4):
                        norm_pair(1, pair)
                if 4 <= s < SLOTS:
                    norm_pair(1, s)
                if s == SLOTS + 3:
                    act.wait_ge(slots_done, (GLU0 + 1) * SLOTS)
                    act.activation(silu[:, :, :], acc[0][:, :, :], ACT.Silu).then_inc(acc_read[0], 1)

            def act_columns(j, c):
                act.activation(act_hi[:, bass.ds(4 * j + 2 * c, 2), :].rearrange("p c t -> p (c t)"),
                               bank[:, c, :], ACT.Copy).then_inc(act_hi_ready, 1)

            with act.Fori(1, GLU) as j:
                for s in range(2 * SLOTS):
                    n = GLU0 * SLOTS + s
                    split_hi(n, s % RING, j * 64 + (16 * 16 + 16 * (n // RING + 1)), j * (2 * SLOTS) + (n - RING + 1))
                    if s in (5, 6):
                        act.wait_ge(act_turned, j)
                        act_columns(j - 1, s - 5)
                    if s == SLOTS + 3:
                        act.wait_ge(slots_done, j * (2 * SLOTS) + (GLU0 + 1) * SLOTS)
                        act.wait_ge(act_turned, j)
                        act.activation(silu[:, :, :], acc[0][:, :, :], ACT.Silu).then_inc(acc_read[0], 1)
            for n in range(DOWN_N0, DOWN_N0 + 4 * DOWN_SLOTS):
                split(n)
                if n == DOWN_N0:
                    act.wait_ge(act_turned, GLU)
                    act_columns(GLU - 1, 0)
                    act_columns(GLU - 1, 1)
                    act.wait_ge(residual_done, 16)
                    load_gamma_beta(A["ln2_g"][0], A["ln2_b"][0])

        @block.vector
        def _(dve):
            steps = [0]

            def then(ins):
                steps[0] += 1
                ins.then_inc(dve_step, 1)
                dve.wait_ge(dve_step, steps[0])

            def split(n, r=None):
                r = n % RING if r is None else r
                dve.wait_ge(hi_ready, n + 1)
                dve.tensor_tensor(w_lo[r][:, :, :], raw[r][:, :, :], w_hi[r][:, :, :],
                                  ALU.subtract).then_inc(lo_ready, 1)

            def row_stats(q, m):
                return dve.bn_stats(stats[:, m, q, :], rows[:, m, q * NB:(q + 1) * NB])

            def finish_stats():
                dve.bn_aggr(mean_var[:, 0, :], stats[:, 0, :, :].rearrange("p q s -> p (q s)"))
                dve.bn_aggr(mean_var[:, 1, :], stats[:, 1, :, :].rearrange("p q s -> p (q s)")).then_inc(var_ready, 1)

            def normalise(q):
                for m in range(TT):
                    part = rows[:, m, q * NB:(q + 1) * NB]
                    ins = dve.tensor_scalar(part, part, mean_var[:, m, 0:1], rstd[:, m:m + 1],
                                            ALU.subtract, ALU.mult)
                ins.then_inc(normed, 1)

            def norm_pair(i, s):
                dve.wait_ge(xT_hi_ready, SLOTS * i + s + 1)
                if SLOTS * i + s >= 2:
                    dve.wait_ge(xT_lo_ready, SLOTS * i + s - 1)
                for c in range(2):
                    col = 2 * KC * i + 2 * s + c
                    ins = dve.tensor_scalar(turned[s % 2][:, c, :], bank[:, s % 4, c * T:(c + 1) * T],
                                            vecT[:, col:col + 1], vecT[:, col + KC:col + KC + 1],
                                            ALU.mult, ALU.add)
                ins.then_inc(turned_ready, 1)
                if s == 0:
                    dve.wait_ge(turned_ready, SLOTS * i + 1)
                    dve.tensor_tensor(xT_lo[:, 0:2, :], turned[0][:, :, :], xT_hi[:, 0:2, :],
                                      ALU.subtract).then_inc(xT_lo_ready, 1)

            def residual(i, m, q):
                cols = slice(q * NB, (q + 1) * NB)
                part = rows[:, m, cols]
                then(dve.scalar_tensor_tensor(part, part, ALPHA, gamma[:, cols], ALU.mult, ALU.mult))
                dve.scalar_tensor_tensor(part, beta[:, cols], ALPHA, part, ALU.mult, ALU.add)\
                   .then_inc(residual_done, 1)

            def add_block(b, q, i):
                a = b % 2
                dve.wait_ge(residual_done, 8 * (i + 1))
                part = rows[:, :, q * NB:(q + 1) * NB]
                ins = dve.tensor_tensor(part, part, acc[a][:, :, :], ALU.add).then_inc(acc_read[a], 1)
                dve.wait_ge(acc_read[a], b // 2 + 1)
                row_stats(q, 0)
                return row_stats(q, 1)

            for i in range(2):
                dve.memset(f[i][:, :, :, 0:1], 0.0)
                dve.memset(f[i][:, :, :, T + 1:T + 2], 0.0)
            dve.memset(heads_in[:, :, :], 0.0)
            dve.memset(scoresT[:, :, :, :], 0.0)

            for q in range(4):
                dve.wait_ge(x_landed[q], 16)
                for m in range(TT):
                    ins = row_stats(q, m)
            then(ins)
            finish_stats()
            dve.wait_ge(vec_turned, 1)
            dve.tensor_copy(vecT[:, :], bank[:, 3, 0:VEC_ROWS]).then_inc(vec_ready, 1)
            dve.wait_ge(rstd_ready, 1)
            normalise(0)
            normalise(1)
            dve.wait_ge(vec_ready, 1)
            split(0)
            norm_pair(0, 0)
            norm_pair(0, 1)
            split(1)
            normalise(2)
            norm_pair(0, 2)
            split(2)
            normalise(3)
            for s in range(3, SLOTS):
                norm_pair(0, s)
                split(s)
            logits = vecT[:, 4 * KC:VEC_ROWS].rearrange("p (d l h) -> p d l h", d=2, l=2)

            def shift_logits():
                then(dve.tensor_tensor(lb_max[:, :, :], logits[:, :, 0, :], logits[:, :, 1, :], ALU.max))
                dve.tensor_tensor(lb_exp[:, :, 0, :], logits[:, :, 0, :], lb_max[:, :, :], ALU.subtract)
                dve.tensor_tensor(lb_exp[:, :, 1, :], logits[:, :, 1, :], lb_max[:, :, :],
                                  ALU.subtract).then_inc(lb_shifted, 1)

            def lower_bounds():
                dve.wait_ge(lb_exped, 1)
                then(dve.tensor_tensor(lb_sum[:, :, :], lb_exp[:, :, 0, :], lb_exp[:, :, 1, :], ALU.add))
                then(dve.reciprocal(lb_sum[:, :, :], lb_sum[:, :, :]))
                then(dve.tensor_tensor(lb[:, :, :], lb_exp[:, :, 0, :], lb_sum[:, :, :], ALU.mult))
                dve.tensor_scalar(one_minus_lb[:, :, :], lb[:, :, :], -1.0, 1.0, ALU.mult, ALU.add)\
                   .then_inc(lb_ready, 1)

            def head_factors(h):
                p, e = h // 2, h % 2
                F = f[p % 2]
                qd = q_dec[h % 2]
                dve.wait_ge(f_ready, 4 * (p + 1))
                dve.wait_ge(qT_ready, p + 1)
                if h:
                    dve.wait_ge(scores_done, h)
                if h >= 2:
                    dve.wait_ge(out_done, h - 1)
                dve.tensor_scalar(k_end[:, :, :], F[:, :, e, 1:T + 1], -1.0, 1.0, ALU.mult, ALU.add)
                dve.tensor_copy(heads_in[:, 0, 0:T:CH], F[:, 0, e, 1:T + 1:CH])
                then(dve.tensor_copy(heads_in[:, 1, CH - 1:T:CH], F[:, 1, e, CH:T + 1:CH]))
                dve.memset(F[:, 0, e, 1:T + 1:CH], 0.0)
                then(dve.memset(F[:, 1, e, CH:T + 1:CH], 0.0))
                dve.tensor_tensor_scan(q_inv[:, 0, :], F[:, 0, e, 1:T + 1], heads_in[:, 0, :], 0.0,
                                       ALU.mult, ALU.add)
                dve.tensor_tensor_scan(q_inv[:, 1, ::-1], F[:, 1, e, T:0:-1], heads_in[:, 1, ::-1], 0.0,
                                       ALU.mult, ALU.add)
                dve.tensor_tensor_scan(qd[:, 0, ::-1], F[:, 0, e, T + 1:1:-1], last_ones[:, ::-1], 0.0,
                                       ALU.mult, ALU.add)
                then(dve.tensor_tensor_scan(qd[:, 1, :], F[:, 1, e, 0:T], first_ones, 0.0,
                                            ALU.mult, ALU.add))

            def head_operands(h):
                p, e = h // 2, h % 2
                qd = q_dec[h % 2]
                dve.tensor_tensor(k_end[:, :, :], k_end[:, :, :], qd[:, :, :], ALU.mult)
                dve.tensor_copy(decay[h % 2][:, 0, :], q_inv[:, 0, CH - 1:T:CH])
                dve.tensor_copy(decay[h % 2][:, 1, :], q_inv[:, 1, 0:T:CH])
                dve.reciprocal(inv_decay[:, 0, :], q_inv[:, 0, CH - 1:T:CH])
                then(dve.reciprocal(inv_decay[:, 1, :], q_inv[:, 1, 0:T:CH]))
                for d in range(2):
                    ins = dve.tensor_tensor(qd[:, d, :], q_inv[:, d, :], qT[p % 2][:, e, :], ALU.mult)
                then(ins)
                for d in range(2):
                    ins = dve.tensor_tensor(q_inv[:, d, :].rearrange("p (c t) -> p c t", t=CH),
                                            qd[:, d, :].rearrange("p (c t) -> p c t", t=CH),
                                            inv_decay[:, d, :].rearrange("p (c a) -> p c a", a=1)
                                            .broadcast_to([P, NCH, CH]), ALU.mult)
                ins.then_inc(head_ready, 1)

            def head_scores(h):
                dve.wait_ge(scores_done, h + 1)
                if h:
                    dve.wait_ge(out_done, h)
                then(dve.copy_predicated(scoresT[:, :, :, :].rearrange("p d m t -> p (d m t)"),
                                         causal.rearrange("p d m t -> p (d m t)"), bank[:, 2, :]))
                dve.tensor_tensor(scores_sum[:, :, :], scoresT[:, 0, :, :], scoresT[:, 1, :, :],
                                  ALU.add).then_inc(scores_ready, 1)

            def head_states(h):
                dve.wait_ge(dstate_done, h + 1)
                if h:
                    dve.wait_ge(out_done, h)
                for d in range(2):
                    then(dve.tensor_copy(state[:, d, 0, :], dstate(d, 0 if d == 0 else 3)))
                    for j in range(1, 3):
                        c = j if d == 0 else 3 - j
                        ins = dve.scalar_tensor_tensor(state[:, d, j, :], state[:, d, j - 1, :],
                                                       decay[h % 2][:, d, c:c + 1], dstate(d, c),
                                                       ALU.mult, ALU.add)
                        if j == 1 or d == 0:
                            then(ins)
                ins.then_inc(states_ready, 1)

            def head_out(h):
                dve.wait_ge(rms_ready, h + 1)
                for m in range(TT):
                    ins = dve.scalar_tensor_tensor(o_heads[:, m, h * P:(h + 1) * P], bank[:, 3, m * P:(m + 1) * P],
                                                   rms[:, m:m + 1], g_norm[:, :], ALU.mult, ALU.mult)
                ins.then_inc(o_ready, 1)

            shift_logits()
            for b in range(1, OUT0 + 1):
                for s in range(SLOTS):
                    split(b * SLOTS + s)
                    if (b, s) == (1, 4):
                        lower_bounds()
                    if b == 1:
                        if s == 0:
                            dve.wait_ge(gb_landed, 32)
                            dve.wait_ge(rows_turned, SLOTS)
                        residual(0, s // 4, s % 4)
                    if b == 2 and s == 0:
                        dve.wait_ge(dft_hi_ready, 1)
                        dve.tensor_tensor(dft_lo[:, :, :], dft_raw[:, :, :], dft_hi[:, :, :],
                                          ALU.subtract).then_inc(dft_ready, 1)
                    if 2 <= b < 10 and b % 2 == 0 and s == 4:
                        p = b // 2 - 1
                        dve.wait_ge(qv_read, 2 * (p + 1))
                        dve.tensor_tensor(tok_q[:, :, :], tok_q[:, :, :], acc[1][:, :, 0:2 * P],
                                          ALU.mult).then_inc(acc_read[1], 1)
                    if 2 <= b < 10 and b % 2 == 0 and s == 7:
                        p = b // 2 - 1
                        dve.wait_ge(q_turned, p + 1)
                        dve.tensor_copy(qT[p % 2][:, :, :].rearrange("p e t -> p (e t)"),
                                        bank[:, 0, :]).then_inc(qT_ready, 1)
                    if 4 <= b < 4 + HEADS and s == 0:
                        head_states(b - 4)
                    if 3 <= b < 3 + HEADS:
                        if s == 1:
                            head_factors(b - 3)
                        if s == 2:
                            head_operands(b - 3)
                        if s == 6:
                            head_scores(b - 3)
                    if 4 <= b < 4 + HEADS and s == 5:
                        head_out(b - 4)
                    if (b, s) in ((9, 4), (10, 7)):
                        i = b - 9
                        dve.wait_ge(u_hi_ready, i + 1)
                        dve.tensor_tensor(u_lo[:, :, :], acc[i][:, :, :], u_hi[:, :, :],
                                          ALU.subtract).then_inc(acc_read[i], 1)
                    if (b, s) in ((9, 7), (10, 6), (11, 5), (12, 3)):
                        g = b - 9
                        dve.wait_ge(dftT_hi_ready, 2 * (g + 1))
                        dve.tensor_tensor(dftT_lo[:, :, 0:T], bank[:, 0:2, 0:T], dftT_hi[:, :, 0:T], ALU.subtract)
                        dve.scalar_tensor_tensor(dftT_lo[:, :, T:2 * T], bank[:, 0:2, T:2 * T], -1.0,
                                                 dftT_hi[:, :, T:2 * T], ALU.mult, ALU.subtract)\
                           .then_inc(dftT_ready, 1)
                    if (b, s) in ((10, 3), (11, 1), (12, 0), (12, 5)):
                        g = ((10, 3), (11, 1), (12, 0), (12, 5)).index((b, s))
                        dve.wait_ge(mix_hi_ready, (1, 2, 3, 6)[g])
                        dve.tensor_tensor(mix_lo[:, 8 + 2 * g:10 + 2 * g, :].rearrange("p c t -> p (c t)"),
                                          bank[:, 0, :],
                                          mix_hi[:, 8 + 2 * g:10 + 2 * g, :].rearrange("p c t -> p (c t)"),
                                          ALU.subtract).then_inc(mix_ready, 1)
                    if (b, s) in ((11, 4), (12, 3)):
                        i = b - 11
                        dve.wait_ge(sig_ready, i + 1)
                        dve.tensor_tensor(tok_z[:, :, :], tok_z[:, :, :], acc[i][:, :, :],
                                          ALU.mult).then_inc(acc_read[i], 1)
                        dve.wait_ge(acc_read[i], 6)
                        dve.wait_ge(o_ready, 4 * (i + 1))
                    if (b, s) in ((11, 5), (12, 4)):
                        i = b - 11
                        dve.tensor_tensor(tok_z[:, :, :], tok_z[:, :, :], o_heads[:, :, i * NB:(i + 1) * NB],
                                          ALU.mult).then_inc(gated, 1)
                    if (b, s) in ((12, 1), (12, 6)):
                        i = (0, 1)[s == 6]
                        for c in range(2):
                            k = 4 * i + 2 * c
                            dve.wait_ge(mix_hi_ready, (4, 7)[i] + c)
                            dve.tensor_tensor(mix_lo[:, k:k + 2, :].rearrange("p c t -> p (c t)"),
                                              bank[:, 2 + c, :],
                                              mix_hi[:, k:k + 2, :].rearrange("p c t -> p (c t)"),
                                              ALU.subtract).then_inc(mix_ready, 1)
            for n in range((OUT0 + 1) * SLOTS, GLU0 * SLOTS):
                split(n)
                if n % SLOTS == 3:
                    b = n // SLOTS - 1
                    dve.wait_ge(slots_done, (b + 1) * SLOTS)
                    add_block(b, b - OUT0, 0)
            for s in range(3):
                split(GLU0 * SLOTS + s)
            dve.wait_ge(slots_done, GLU0 * SLOTS)
            then(add_block(GLU0 - 1, 3, 0))
            finish_stats()
            dve.wait_ge(rstd_ready, 2)
            normalise(0)
            normalise(1)
            norm_pair(1, 0)
            norm_pair(1, 1)
            normalise(2)
            split(GLU0 * SLOTS + 3)
            norm_pair(1, 2)
            normalise(3)
            norm_pair(1, 3)
            for s in range(4, SLOTS):
                split(GLU0 * SLOTS + s)
                norm_pair(1, s)
            dve.wait_ge(gb_landed, 64)
            dve.wait_ge(rows_turned, 2 * SLOTS)
            for s in range(SLOTS):
                split((GLU0 + 1) * SLOTS + s)
                residual(1, s // 4, s % 4)

            def glu(j):
                dve.wait_ge(acc_read[0], j + (GLU0 // 2 + 1))
                dve.wait_ge(slots_done, j * (2 * SLOTS) + (GLU0 + 2) * SLOTS)
                dve.tensor_tensor(silu[:, :, :], silu[:, :, :], acc[1][:, :, :], ALU.mult).then_inc(acc_read[1], 1)

            def act_columns(j, c):
                cols = act_hi[:, bass.ds(4 * j + 2 * c, 2), :].rearrange("p c t -> p (c t)")
                low = act_lo[:, bass.ds(4 * j + 2 * c, 2), :].rearrange("p c t -> p (c t)")
                dve.wait_ge(act_hi_ready, 2 * j + c + 1)
                dve.tensor_tensor(low, bank[:, c, :], cols, ALU.subtract).then_inc(act_ready, 1)

            with dve.Fori(1, GLU) as j:
                for s in range(2 * SLOTS):
                    split(j * (2 * SLOTS) + (GLU0 * SLOTS + s), s % RING)
                    if s == 3:
                        glu(j - 1)
                    if s in (5, 6):
                        act_columns(j - 1, s - 5)
            split(DOWN_N0)
            glu(GLU - 1)
            act_columns(GLU - 1, 0)
            act_columns(GLU - 1, 1)
            for n in range(1, 4 * DOWN_SLOTS):
                split(DOWN_N0 + n)
                if n > DOWN_SLOTS and n % DOWN_SLOTS == 3:
                    b = n // DOWN_SLOTS - 1
                    dve.wait_ge(slots_done, DOWN_N0 + (b + 1) * DOWN_SLOTS)
                    add_block(DOWN0 + b, b, 1)
            dve.wait_ge(slots_done, DOWN_N0 + 4 * DOWN_SLOTS)
            then(add_block(DOWN0 + 3, 3, 1))
            finish_stats()
            dve.wait_ge(gb_landed, 96)
            dve.wait_ge(rstd_ready, 3)
            for q in range(4):
                cols = slice(q * NB, (q + 1) * NB)
                for m in range(TT):
                    part = rows[:, m, cols]
                    ins = dve.scalar_tensor_tensor(part, part, mean_var[:, m, 0:1], gamma[:, cols],
                                                   ALU.subtract, ALU.mult)
                then(ins)
                for m in range(TT):
                    part = rows[:, m, cols]
                    dve.scalar_tensor_tensor(part, part, rstd[:, m:m + 1], beta[:, cols],
                                             ALU.mult, ALU.add).then_inc(out_ready, 1)

        @block.tensor
        def _(pe):
            def slot(n, r, a, left_hi, left_lo, k0, first, last):
                pe.wait_ge(lo_ready, n + 1)
                for c in range(2):
                    k = k0 + c
                    for m in range(TT):
                        out = acc[a][:, m, :]
                        hi, lo = left_hi[:, k, m * P:(m + 1) * P], left_lo[:, k, m * P:(m + 1) * P]
                        pe.matmul(out, hi, w_hi[r][:, c, :], start=(first and c == 0), stop=False)
                        pe.matmul(out, hi, w_lo[r][:, c, :], start=False, stop=False)
                        ins = pe.matmul(out, lo, w_hi[r][:, c, :], start=False, stop=(last and c == 1))
                ins.then_inc(slots_done, 1)

            def turn_rows(i, s):
                if i == 0 and s == 3:
                    pe.wait_ge(vec_ready, 1)
                pe.wait_ge(normed, 4 * i + s // 2 + 1)
                if s >= 4:
                    pe.wait_ge(turned_ready, SLOTS * i + s - 3)
                for c in range(2):
                    k = 2 * s + c
                    for m in range(TT):
                        ins = pe.transpose(bank[:, s % 4, c * T + m * P:c * T + (m + 1) * P],
                                           rows[:, m, k * P:(k + 1) * P], ident[:, :])
                ins.then_inc(rows_turned, 1)

            def turn(b, cols, source, done):
                for t in range(2):
                    for m in range(TT):
                        ins = pe.transpose(bank[:, b, t * T + m * P:t * T + (m + 1) * P],
                                           source[:, m, cols + t * P:cols + (t + 1) * P], ident[:, :])
                if done is not None:
                    ins.then_inc(done, 1)

            def head_scores(h):
                p, e = h // 2, h % 2
                pe.wait_ge(head_ready, h + 1)
                if h:
                    pe.wait_ge(o_ready, h)
                for d in range(2):
                    for m in range(TT):
                        ins = pe.transpose(bank[:, 3, (2 * d + m) * P:(2 * d + m + 1) * P],
                                           k_end[:, d, m * P:(m + 1) * P], ident[:, :])
                ins.then_inc(k_turned, 1)
                for d in range(2):
                    for m in range(TT):
                        ins = pe.matmul(bank[:, 2, (2 * d + m) * P:(2 * d + m + 1) * P],
                                        k_end[:, d, m * P:(m + 1) * P], q_inv[:, d, m * P:(m + 1) * P],
                                        start=True, stop=True)
                ins.then_inc(scores_done, 1)

            def head_dstates(h):
                p, e = h // 2, h % 2
                pe.wait_ge(k_rows_ready, h + 1)
                pe.wait_ge(scores_ready, h + 1)
                for d, c in ((0, 0), (0, 1), (0, 2), (1, 3), (1, 2), (1, 1)):
                    part = slice(CH * (c % 2), CH * (c % 2) + CH)
                    ins = pe.matmul(dstate(d, c), k_rows[part, d, c // 2, :],
                                    v[p % 2][part, c // 2, e * P:(e + 1) * P], start=True, stop=True)
                ins.then_inc(dstate_done, 1)

            def head_out(h):
                p, e = h // 2, h % 2
                pe.wait_ge(states_ready, h + 1)
                for m in range(TT):
                    vals = v[p % 2][:, m, e * P:(e + 1) * P]
                    pe.matmul(bank[:, 3, m * P:(m + 1) * P], scores_sum[:, m, :], vals, start=True, stop=False,
                              skip_group_check=True)
                    for c in (2 * m, 2 * m + 1):
                        out = bank[CH * (c % 2):CH * (c % 2) + CH, 3, m * P:(m + 1) * P]
                        for d, j in ((0, c - 1), (1, 2 - c)):
                            if j >= 0:
                                ins = pe.matmul(out, q_dec[h % 2][:, d, c * CH:(c + 1) * CH], state[:, d, j, :],
                                                start=False, stop=True, skip_group_check=True)
                ins.then_inc(out_done, 1)

            def fourier_tokens(g):
                col = (g % 2) * T
                for gt in range(2):
                    for tc in range(TT):
                        hi = u_hi[:, tc, col + gt * P:col + (gt + 1) * P]
                        lo = u_lo[:, tc, col + gt * P:col + (gt + 1) * P]
                        pe.matmul(bank[:, gt, :], hi, dft_hi[:, tc, :], start=(tc == 0), stop=False)
                        pe.matmul(bank[:, gt, :], hi, dft_lo[:, tc, :], start=False, stop=False)
                        ins = pe.matmul(bank[:, gt, :], lo, dft_hi[:, tc, :], start=False, stop=(tc == 1))
                ins.then_inc(four1_done, 1)

            def fourier_channels(g):
                pe.wait_ge(dftT_ready, g + 1)
                for ct in range(2):
                    out = bank[:, 0, ct * T:(ct + 1) * T]
                    for i in range(4):
                        part, gt = i // 2, i % 2
                        cols = slice(part * T + ct * P, part * T + (ct + 1) * P)
                        mov = slice(part * T, (part + 1) * T)
                        pe.matmul(out, dft_hi[:, gt, cols], dftT_hi[:, gt, mov], start=(i == 0), stop=False)
                        pe.matmul(out, dft_hi[:, gt, cols], dftT_lo[:, gt, mov], start=False, stop=False)
                        ins = pe.matmul(out, dft_lo[:, gt, cols], dftT_hi[:, gt, mov], start=False, stop=(i == 3))
                ins.then_inc(four2_done, 1)

            pe.wait_ge(vec_landed, 16 * 6)
            pe.wait_ge(ident_landed, 16)
            pe.transpose(bank[:, 3, 0:VEC_ROWS], vec_rows[:, :], ident[0:VEC_ROWS, 0:VEC_ROWS]).then_inc(vec_turned, 1)

            for s in range(4):
                turn_rows(0, s)
            for b in range(OUT0):
                if b >= 2:
                    pe.wait_ge(acc_read[b % 2], b // 2)
                for s in range(SLOTS):
                    if b == 0:
                        pe.wait_ge(xT_lo_ready, s + 1)
                    slot(b * SLOTS + s, s % RING, b % 2, xT_hi, xT_lo, 2 * s, s == 0, s == SLOTS - 1)
                    if b == 0 and s < 4:
                        turn_rows(0, s + 4)
                    if b < 9 and b % 2 == 1 and s == 3:
                        p = b // 2
                        pe.wait_ge(acc_read[0], p + 1)
                        if p:
                            pe.wait_ge(qT_ready, p)
                        else:
                            pe.wait_ge(xT_lo_ready, SLOTS)
                        turn(0, 0, tok_z, None)
                        turn(1, 2 * P, tok_z, z_turned)
                    if 2 <= b < 10 and b % 2 == 0 and s == 3:
                        p = b // 2 - 1
                        pe.wait_ge(acc_read[1], p + 1)
                        pe.wait_ge(f_ready, 4 * (p + 1))
                        turn(0, 0, tok_q, q_turned)
                    if 4 <= b < 4 + HEADS and s == 1:
                        head_out(b - 4)
                    if 3 <= b < 3 + HEADS:
                        if s == 4:
                            head_scores(b - 3)
                        if s == 6:
                            head_dstates(b - 3)
                    if (b, s) == (9, 4):
                        pe.wait_ge(acc_read[0], 5)
                        pe.wait_ge(dft_ready, 1)
                        fourier_tokens(0)
                    if (b, s) == (10, 0):
                        fourier_channels(0)
                    if (b, s) == (10, 3):
                        pe.wait_ge(mix_ready, 1)
                        fourier_tokens(1)
                    if (b, s) == (10, 7):
                        fourier_channels(1)
                    if (b, s) == (11, 2):
                        pe.wait_ge(mix_ready, 2)
                        pe.wait_ge(acc_read[1], 5)
                        fourier_tokens(2)
                    if (b, s) == (11, 5):
                        fourier_channels(2)
                    if (b, s) == (11, 6):
                        pe.wait_ge(gated, 1)
                        pe.wait_ge(o_ready, HEADS)
                        turn(2, 0, tok_z, None)
                        turn(3, 2 * P, tok_z, gated_turned)

            pe.wait_ge(acc_read[0], 6)
            for s in range(SLOTS):
                pe.wait_ge(mix_ready, s + 1)
                slot(OUT0 * SLOTS + s, s % RING, 0, mix_hi, mix_lo, MIX_ORDER[s], s == 0, s == SLOTS - 1)
                if s == 0:
                    pe.wait_ge(mix_ready, 3)
                    fourier_tokens(3)
                if s == 3:
                    fourier_channels(3)
                if s == 4:
                    pe.wait_ge(gated, 2)
                    pe.wait_ge(mix_ready, 5)
                    turn(2, 0, tok_z, None)
                    turn(3, 2 * P, tok_z, gated_turned)
            for b in range(OUT0 + 1, GLU0):
                pe.wait_ge(acc_read[b % 2], b // 2)
                for s in range(SLOTS):
                    slot(b * SLOTS + s, s % RING, b % 2, mix_hi, mix_lo, MIX_ORDER[s], s == 0, s == SLOTS - 1)

            for s in range(4):
                turn_rows(1, s)
            for b in (GLU0, GLU0 + 1):
                pe.wait_ge(acc_read[b % 2], b // 2)
                for s in range(SLOTS):
                    if b == GLU0:
                        pe.wait_ge(xT_lo_ready, SLOTS + s + 1)
                    slot(b * SLOTS + s, s % RING, b % 2, xT_hi, xT_lo, 2 * s, s == 0, s == SLOTS - 1)
                    if b == GLU0 and s < 4:
                        turn_rows(1, s + 4)

            def turn_act(j):
                pe.wait_ge(acc_read[1], j + (GLU0 // 2 + 1))
                turn(0, 0, silu, None)
                turn(1, 2 * P, silu, act_turned)

            with pe.Fori(1, GLU) as j:
                for a in range(2):
                    pe.wait_ge(acc_read[a], j + GLU0 // 2)
                    for s in range(SLOTS):
                        slot(j * (2 * SLOTS) + ((GLU0 + a) * SLOTS + s), s % RING, a, xT_hi, xT_lo, 2 * s,
                             s == 0, s == SLOTS - 1)
                        if a == 0 and s == 3:
                            turn_act(j - 1)
            turn_act(GLU - 1)
            with pe.Fori(0, 2) as i:
                for a in range(2):
                    pe.wait_ge(acc_read[a], i + DOWN0 // 2)
                    for s in range(DOWN_SLOTS):
                        n = a * DOWN_SLOTS + s
                        if n == DOWN_SLOTS - 2:
                            pe.wait_ge(act_ready, 2 * GLU)
                        slot(i * (2 * DOWN_SLOTS) + (DOWN_N0 + n), n % RING, a, act_hi, act_lo, 2 * s,
                             s == 0, s == DOWN_SLOTS - 1)


def kernel(**inputs):
    import numpy as np
    import concourse.bacc as bacc
    from concourse.bass_utils import run_bass_kernel_spmd

    t = np.arange(T)
    first = np.tile((t % CH == 0).astype(np.float32), (P, 1))
    last = np.tile((t % CH == CH - 1).astype(np.float32), (P, 1))
    s_, t_ = np.arange(P)[:, None], np.arange(P)[None, :]
    same = s_ // CH == t_ // CH
    masks = [(same & (s_ <= t_)).astype(np.float32), (same & (s_ >= t_)).astype(np.float32)]
    consts = np.concatenate([np.eye(P, dtype=np.float32), first, last] + [m for m in masks for _ in range(TT)], axis=1)
    angle = 2.0 * np.pi * (np.outer(t, t) % T) / T
    dft = np.concatenate([np.cos(angle), np.sin(angle)], axis=1) / 16.0

    nc = bacc.Bacc("TRN2", target_bir_lowering=False, num_devices=1)
    arrays = {name: np.ascontiguousarray(a) for name, a in inputs.items()}
    arrays["consts"] = np.ascontiguousarray(consts, dtype=np.float32)
    arrays["dft"] = np.ascontiguousarray(dft, dtype=np.float32)
    A, feeds = {}, {}
    for name, a in arrays.items():
        A[name] = nc.dram_tensor(f"in_{name}", a.shape, mybir.dt.from_np(a.dtype), kind="ExternalInput").ap()
        feeds[f"in_{name}"] = a
    A["out"] = nc.dram_tensor("out_x", (1, T, D), F32, kind="ExternalOutput").ap()
    build(nc, A)
    r = run_bass_kernel_spmd(nc, [feeds], core_ids=[0])
    return r.results[0]["out_x"]
```

```python
import math
from contextlib import ExitStack

import concourse.bass as bass
from concourse import mybir

F32 = mybir.dt.float32
F32R = mybir.dt.float32r
BF16 = mybir.dt.bfloat16
U32 = mybir.dt.uint32
ALU = mybir.AluOpType
ACT = mybir.ActivationFunctionType

P = 128
T = 256
TT = T // P
D = 2048
KC = D // P
NB = 512
HEADS = 8
CH = 64
NCH = T // CH
FF = int(math.ceil((8 * D / 3) / 256) * 256)
FC = FF // P
GLU = FF // NB
RING = 4
SLOTS = KC // 2
DOWN_SLOTS = FC // 2
OUT0 = 12
GLU0 = 16
DOWN0 = GLU0 + 2 * GLU
DOWN_N0 = DOWN0 * SLOTS
ALPHA = 2.0 ** 0.25
LN_EPS = 1e-5
RMS_EPS = 1e-6
MIX_ORDER = [8, 10, 12, 14, 0, 2, 4, 6]
STATS = 6
HALF = T // 2 + 1
OWN = D - 640
VEC_ROWS = 96
SBUF_START = 16 * 1024 + 512
SBUF_END = 224 * 1024


def build(nc, A):
    with ExitStack() as ctx:
        place = {"at": SBUF_START}

        def sb(name, shape, dt=F32, at=None):
            size = 4 * math.prod(shape[1:])
            if at is None:
                at = place["at"]
                place["at"] += (size + 31) // 32 * 32
            return nc.alloc_sbuf_tensor_at(name, shape, dt, offset=at)

        def sem(name):
            return ctx.enter_context(nc.semaphore(name))

        rows = sb("rows", [P, TT, D])
        xT_hi = sb("xT_hi", [P, KC, T], F32R)
        xT_lo = sb("xT_lo", [P, KC, T], F32R)
        raw = [sb(f"raw{i}", [P, 2, NB]) for i in range(RING)]
        w_hi = [sb(f"w_hi{i}", [P, 2, NB], F32R) for i in range(RING)]
        w_lo = [sb(f"w_lo{i}", [P, 2, NB], F32R) for i in range(RING)]
        vecT = sb("vecT", [P, VEC_ROWS])
        mean_var = sb("mean_var", [P, TT, 2])
        stats = sb("stats", [P, TT, 4, STATS])
        var_eps = sb("var_eps", [P, TT])
        rstd = sb("rstd", [P, TT])
        minus_half = sb("minus_half", [P, 1])
        shift = sb("shift", [P, TT])
        ident = sb("ident", [P, P])
        region = place["at"]
        mix_hi = sb("mix_hi", [P, KC, T], F32R)
        mix_lo = sb("mix_lo", [P, KC, T], F32R)
        consts = sb("consts", [P, 4 * T])
        tok_z = sb("tok_z", [P, TT, NB])
        tok_q = sb("tok_q", [P, TT, 2 * P])
        v = [sb(f"v{i}", [P, TT, 2 * P]) for i in range(2)]
        f = [sb(f"f{i}", [P, 2, 2, T + 2]) for i in range(2)]
        qT = [sb(f"qT{i}", [P, 2, T]) for i in range(2)]
        o_heads_at = place["at"]
        o_heads = sb("o_heads", [P, TT, HEADS * P])
        turned = [sb(f"turned{i}", [P, 2, T], at=place["at"] + 8 * T * i) for i in range(2)]
        k_end = sb("k_end", [P, 2, T])
        q_inv = sb("q_inv", [P, 2, T])
        q_dec = [sb(f"q_dec{i}", [P, 2, T]) for i in range(2)]
        heads_in = sb("heads_in", [P, 2, T])
        k_rows = sb("k_rows", [P, 2, TT, P])
        scoresT = sb("scoresT", [P, 2, TT, P])
        scores_sum = sb("scores_sum", [P, TT, P])
        state = sb("state", [P, 2, 3, P])
        squares = sb("squares", [P, P])
        g_norm = sb("g_norm", [P, P])
        decay = [sb(f"decay{i}", [P, 2, NCH]) for i in range(2)]
        inv_decay = sb("inv_decay", [P, 2, NCH])
        ssq = sb("ssq", [P, TT])
        rms_in = sb("rms_in", [P, TT])
        rms = sb("rms", [P, TT])
        lb_max = sb("lb_max", [P, 2, HEADS])
        lb_exp = sb("lb_exp", [P, 2, 2, HEADS])
        lb_sum = sb("lb_sum", [P, 2, HEADS])
        lb = sb("lb", [P, 2, HEADS])
        one_minus_lb = sb("one_minus_lb", [P, 2, HEADS])
        dft_hi = sb("dft_hi", [P, TT, 2 * T], F32R)
        dft_lo = sb("dft_lo", [P, TT, 2 * T], F32R)
        four = place["at"]
        u_hi = sb("u_hi", [P, TT, NB], F32R)
        u_lo = sb("u_lo", [P, TT, NB], F32R)
        dftT_at = place["at"]
        dftT_hi = sb("dftT_hi", [P, 2, 2 * T], F32R)
        dftT_lo = sb("dftT_lo", [P, 2, 2 * T], F32R)
        halves = sb("halves", [P, 2, 2 * T], at=dftT_at)
        four_out = sb("four_out", [P, 2, 2, T], at=dftT_at + 4 * 4 * T)
        dft_raw = sb("dft_raw", [P, TT, 2 * T], at=o_heads_at)
        vec_rows = sb("vec_rows", [VEC_ROWS, P], at=o_heads_at + 4 * TT * 2 * T)
        place["at"] = region
        act_hi = sb("act_hi", [P, FC, T], F32R)
        act_lo = sb("act_lo", [P, FC, T], F32R)
        silu = sb("silu", [P, TT, NB])
        gb_at = max(place["at"], four)
        gamma = sb("gamma", [P, D], at=gb_at)
        beta = sb("beta", [P, D], at=gb_at + 4 * D)

        assert max(place["at"], gb_at + 8 * D) <= SBUF_END, (place["at"], gb_at + 8 * D)

        first_ones = consts[:, 0:T]
        last_ones = consts[:, T:2 * T]
        causal = consts[:, 2 * T:4 * T].bitcast(U32).rearrange("p (d m t) -> p d m t", d=2, m=TT)

        acc = [ctx.enter_context(nc.psum_tensor(f"acc{i}", [P, TT, NB], F32)) for i in range(2)]
        bank = ctx.enter_context(nc.psum_tensor("bank", [P, 4, NB], F32))

        def dstate(d, c):
            at = {(0, 0): 0, (0, 2): 1, (1, 2): 2, (0, 1): 0, (1, 1): 1, (1, 3): 2}[d, c]
            return bank[:, 3 - c % 2, at * P:(at + 1) * P]

        SINES = T - HALF
        COSINES = 2 * HALF

        def by_group(tile, first, end):
            return tile[:, :, first:end].rearrange("p c (g t) -> p g c t", g=2)

        made = bank[:, 0:2, :].rearrange("p g (c t) -> p g c t", c=2)
        made_cosines, made_sines = made[:, :, :, SINES:T], made[:, :, :, 0:SINES]

        x_landed = [sem(f"x_landed{i}") for i in range(4)]
        vec_landed = sem("vec_landed")
        ident_landed = sem("ident_landed")
        consts_landed = sem("consts_landed")
        gb_landed = sem("gb_landed")
        slot_landed = [sem(f"slot_landed{i}") for i in range(RING)]
        hi_ready = sem("hi_ready")
        lo_ready = sem("lo_ready")
        slots_done = sem("slots_done")
        acc_read = [sem("acc_read0"), sem("acc_read1")]
        fills_done = sem("fills_done")
        vec_turned = sem("vec_turned")
        vec_ready = sem("vec_ready")
        lb_shifted = sem("lb_shifted")
        lb_exped = sem("lb_exped")
        lb_ready = sem("lb_ready")
        dft_hi_ready = sem("dft_hi_ready")
        pool_step = sem("pool_step")
        var_ready = sem("var_ready")
        rstd_ready = sem("rstd_ready")
        normed = sem("normed")
        rows_turned = sem("rows_turned")
        xT_hi_ready = sem("xT_hi_ready")
        turned_ready = sem("turned_ready")
        xT_lo_ready = sem("xT_lo_ready")
        first_lo_ready = sem("first_lo_ready")
        first_tile_done = sem("first_tile_done")
        shift_ready = sem("shift_ready")
        scaled = sem("scaled")
        assisted = sem("assisted")
        z_turned = sem("z_turned")
        f_ready = sem("f_ready")
        qv_read = sem("qv_read")
        q_turned = sem("q_turned")
        qT_ready = sem("qT_ready")
        head_ready = sem("head_ready")
        k_turned = sem("k_turned")
        scores_done = sem("scores_done")
        k_rows_ready = sem("k_rows_ready")
        scores_ready = sem("scores_ready")
        dstate_done = sem("dstate_done")
        states_ready = sem("states_ready")
        out_done = sem("out_done")
        ssq_ready = sem("ssq_ready")
        rms_ready = sem("rms_ready")
        o_ready = sem("o_ready")
        sig_ready = sem("sig_ready")
        gated = sem("gated")
        gated_turned = sem("gated_turned")
        u_hi_ready = sem("u_hi_ready")
        four1_done = sem("four1_done")
        dftT_hi_ready = sem("dftT_hi_ready")
        dftT_ready = sem("dftT_ready")
        four2_done = sem("four2_done")
        halves_ready = sem("halves_ready")
        four_ready = sem("four_ready")
        mix_hi_ready = sem("mix_hi_ready")
        mix_ready = sem("mix_ready")
        residual_done = sem("residual_done")
        dft_ready = sem("dft_ready")
        act_turned = sem("act_turned")
        act_hi_ready = sem("act_hi_ready")
        act_ready = sem("act_ready")
        dve_step = sem("dve_step")
        out_ready = sem("out_ready")
        out_landed = sem("out_landed")

        x_rows = A["x"][0].rearrange("(m p) d -> p m d", p=P)
        out_rows = A["out"][0].rearrange("(m p) d -> m p d", p=P)
        w_in = A["w_in"][0]
        win_pairs = w_in.rearrange("(s c p) (m z n) -> s m p c z n", c=2, p=P, z=2, n=1024)
        win_cols = w_in.rearrange("(s c p) n -> s p c n", c=2, p=P)
        wout_cols = A["w_out"][0].rearrange("(s c p) n -> s p c n", c=2, p=P)
        wgate_cols = A["w_gate"][0].rearrange("(s c p) n -> s p c n", c=2, p=P)
        wup_cols = A["w_up"][0].rearrange("(s c p) n -> s p c n", c=2, p=P)
        wdown_cols = A["w_down"][0].rearrange("(s c p) n -> s p c n", c=2, p=P)

        block = ctx.enter_context(nc.Block())

        @block.sync
        def _(sp):
            for q in range(4):
                sp.dma_start(rows[:, :, q * NB:(q + 1) * NB],
                             x_rows[:, :, q * NB:(q + 1) * NB]).then_inc(x_landed[q], 16)

            def load_pair(head_pair, n0, first):
                for which in range(2):
                    for s in range(SLOTS):
                        n = which * SLOTS + s
                        r = s % RING
                        dst = raw[r][:, :, :].rearrange("p c (z n) -> p c z n", z=2)
                        for c in range(2):
                            src = win_pairs[s, 1 - which, :, c, :, bass.ds(head_pair, 2 * P)]
                            if c == 0 and not (first and n < RING):
                                sp.wait_ge(lo_ready, n0 + (n - RING + 1))
                            sp.dma_start(dst[:, c], src).then_inc(slot_landed[r], 16)

            def load(src, dst_slot, freed):
                sp.wait_ge(lo_ready, freed)
                sp.dma_start(raw[dst_slot][:, :, :], src).then_inc(slot_landed[dst_slot], 16)

            load_pair(0, 0, True)
            with sp.Fori(2, 5) as i:
                load_pair(i * (2 * P) - 2 * P, i * (2 * SLOTS) - 2 * SLOTS, False)
            for b in range(8, OUT0):
                col = 5 * 1024 + (b - 8) * NB if b < 10 else 4 * 1024 + (b - 10) * NB
                for s in range(SLOTS):
                    load(win_cols[s, :, :, col:col + NB], s % RING, b * SLOTS + s - RING + 1)
            with sp.Fori(1, D // NB + 1) as i:
                col = i * NB - NB
                for s in range(SLOTS):
                    load(wout_cols[MIX_ORDER[s] // 2, :, :, bass.ds(col, NB)], s % RING,
                         i * SLOTS + ((OUT0 - 1) * SLOTS + s - RING + 1))
            with sp.Fori(0, GLU) as i:
                col = sp.snap(i * NB)
                for which, cols in enumerate((wgate_cols, wup_cols)):
                    for s in range(SLOTS):
                        load(cols[s, :, :, bass.ds(col, NB)], s % RING,
                             i * (2 * SLOTS) + ((GLU0 + which) * SLOTS + s - RING + 1))
            with sp.Fori(0, D // NB // 2) as i:
                col = sp.snap(i * (2 * NB))
                for half in range(2):
                    for s in range(DOWN_SLOTS):
                        n = half * DOWN_SLOTS + s
                        load(wdown_cols[s, :, :, bass.ds(col + half * NB, NB)], n % RING,
                             i * (2 * DOWN_SLOTS) + (DOWN_N0 + n - RING + 1))
            for m in range(TT):
                for q in range(4):
                    cols = slice(q * NB, min((q + 1) * NB, OWN)) if q < 3 else slice(OWN, D)
                    if q < 3:
                        sp.wait_ge(out_ready, 3 * m + q + 1)
                    else:
                        sp.wait_ge(assisted, m + 1)
                    sp.dma_start(out_rows[m][:, cols], rows[:, m, cols]).then_inc(out_landed, 16)
            sp.wait_ge(out_landed, 16 * 4 * TT)

        @block.gpsimd
        def _(pool):
            steps = [0]

            def then(ins):
                steps[0] += 1
                ins.then_inc(pool_step, 1)
                pool.wait_ge(pool_step, steps[0])

            then(pool.memset(minus_half[:, :], -0.5))

            def layer_norm_rstd(i):
                for m in range(TT):
                    pool.wait_ge(var_ready, TT * i + m + 1)
                    then(pool.tensor_scalar(var_eps[:, m:m + 1], mean_var[:, m, 1:2], 1.0, LN_EPS,
                                            ALU.mult, ALU.add))
                    pool.tensor_tensor(rstd[:, m:m + 1], var_eps[:, m:m + 1], minus_half[:, :],
                                       ALU.pow).then_inc(rstd_ready, 1)

            def xT_lows(i):
                for s in range(1, SLOTS):
                    pool.wait_ge(turned_ready, SLOTS * i + s + 1)
                    pool.tensor_tensor(xT_lo[:, 2 * s:2 * s + 2, :], turned[s % 2][:, :, :],
                                       xT_hi[:, 2 * s:2 * s + 2, :], ALU.subtract).then_inc(xT_lo_ready, 1)

            layer_norm_rstd(0)
            xT_lows(0)
            for h in range(HEADS):
                pool.wait_ge(ssq_ready, 2 * (h + 1))
                then(pool.tensor_scalar(rms_in[:, :], ssq[:, :], 1.0 / P, RMS_EPS, ALU.mult, ALU.add))
                pool.tensor_tensor(rms[:, :], rms_in[:, :], minus_half[:, 0:1].broadcast_to([P, TT]),
                                   ALU.pow).then_inc(rms_ready, 1)
            layer_norm_rstd(1)
            xT_lows(1)
            layer_norm_rstd(2)
            pool.wait_ge(gb_landed, 96)
            for m in range(TT):
                part = rows[:, m, OWN:D]
                pool.wait_ge(scaled, m + 1)
                then(pool.tensor_tensor(part, part, gamma[:, OWN:D], ALU.mult))
                pool.tensor_tensor(part, part, beta[:, OWN:D], ALU.add).then_inc(assisted, 1)

        @block.scalar
        def _(act):
            vec_src = [A["ln_emb_g"], A["ln_emb_b"], A["ln1_g"][0], A["ln1_b"][0]]
            for i, a in enumerate(vec_src):
                act.dma_start(vec_rows[i * KC:(i + 1) * KC, :],
                              a.rearrange("(k p) -> k p", p=P)).then_inc(vec_landed, 16)
            for i, a in enumerate((A["lb_fwd_logits"], A["lb_bwd_logits"])):
                act.dma_start(vec_rows[4 * KC + 16 * i:4 * KC + 16 * (i + 1), :],
                              a.rearrange("l (h p) -> (l h) p", p=P)).then_inc(vec_landed, 16)
            act.dma_start(ident[:, :], A["consts"][:, 0:P]).then_inc(ident_landed, 16)

            def load_gamma_beta(g, b):
                for dst, src in ((gamma, g), (beta, b)):
                    act.dma_start(dst[:, :], src.rearrange("(a d) -> a d", a=1).broadcast_to([P, D]))\
                       .then_inc(gb_landed, 16)

            def load_constants():
                act.dma_start(consts[:, :], A["consts"][:, P:]).then_inc(consts_landed, 16)
                act.dma_start(dft_raw[:, :, :], A["dft"].rearrange("(m p) n -> p m n", p=P))\
                   .then_inc(consts_landed, 16)
                act.dma_start(g_norm[:, :], A["g_norm"].broadcast_to([P, P])).then_inc(consts_landed, 16)

            def split_hi(n, r, landed, used=None):
                act.wait_ge(slot_landed[r], landed)
                if used is not None:
                    act.wait_ge(slots_done, used)
                act.activation(w_hi[r][:, :, :], raw[r][:, :, :], ACT.Copy).then_inc(hi_ready, 1)

            def split(n):
                r, turn = n % RING, n // RING
                landed = 32 * (turn + 1) if n < 64 else 32 * 16 + 16 * (turn - 15)
                split_hi(n, r, landed, n - RING + 1 if n >= RING else None)

            def norm_pair(i, s):
                act.wait_ge(rows_turned, SLOTS * i + s + 1)
                for c in range(2):
                    k = 2 * s + c
                    col = 2 * KC * i + k
                    ins = act.activation(xT_hi[:, k, :], bank[:, s % 4, c * T:(c + 1) * T], ACT.Identity,
                                         bias=vecT[:, col + KC:col + KC + 1], scale=vecT[:, col:col + 1])
                ins.then_inc(xT_hi_ready, 1)

            split(0)
            split(1)
            act.wait_ge(vec_ready, 1)
            norm_pair(0, 0)
            norm_pair(0, 1)
            load_gamma_beta(A["ln_emb_g"], A["ln_emb_b"])
            for s in range(2, SLOTS):
                norm_pair(0, s)
                split(s)
                if s == 2:
                    load_constants()
            for b in range(1, OUT0 + 1):
                for s in range(SLOTS):
                    split(b * SLOTS + s)
                    if (b, s) == (1, 0):
                        act.wait_ge(lb_shifted, 1)
                        act.activation(lb_exp[:, :, :, :], lb_exp[:, :, :, :], ACT.Exp).then_inc(lb_exped, 1)
                    if (b, s) == (2, 0):
                        act.wait_ge(consts_landed, 48)
                        act.activation(dft_hi[:, :, :], dft_raw[:, :, :], ACT.Copy).then_inc(dft_hi_ready, 1)
                    if b < 9 and b % 2 == 1 and s == 3:
                        p = b // 2
                        act.wait_ge(slots_done, b * SLOTS)
                        if p:
                            act.wait_ge(z_turned, p)
                        act.activation(tok_z[:, :, :], acc[0][:, :, :], ACT.Sigmoid).then_inc(acc_read[0], 1)
                    if b < 9 and b % 2 == 1 and s in (6, 7):
                        p, d = b // 2, s - 6
                        act.wait_ge(z_turned, p + 1)
                        if p >= 2:
                            act.wait_ge(head_ready, 2 * p - 2)
                        if p == 0:
                            act.wait_ge(lb_ready, 1)
                        for e in range(2):
                            h = 2 * p + e
                            ins = act.activation(f[p % 2][:, d, e, 1:T + 1], bank[:, d, e * T:(e + 1) * T],
                                                 ACT.Identity, bias=lb[:, d, h:h + 1],
                                                 scale=one_minus_lb[:, d, h:h + 1])
                            ins.then_inc(f_ready, 1)
                    if 2 <= b < 10 and b % 2 == 0 and s == 3:
                        p = b // 2 - 1
                        act.wait_ge(slots_done, b * SLOTS)
                        if p:
                            act.wait_ge(q_turned, p)
                        act.activation(tok_q[:, :, :], acc[1][:, :, 0:2 * P], ACT.Sigmoid).then_inc(qv_read, 1)
                        if p >= 2:
                            act.wait_ge(out_done, 2 * p - 2)
                        act.activation(v[p % 2][:, :, :], acc[1][:, :, 2 * P:4 * P], ACT.Copy).then_inc(qv_read, 1)
                    if 3 <= b < 3 + HEADS and s == 6:
                        h = b - 3
                        act.wait_ge(k_turned, h + 1)
                        if h:
                            act.wait_ge(dstate_done, h)
                        act.activation(k_rows[:, :, :, :].rearrange("p d m k -> p (d m k)"),
                                       bank[:, 3, :], ACT.Copy).then_inc(k_rows_ready, 1)
                    if 4 <= b < 4 + HEADS and s == 4:
                        h = b - 4
                        act.wait_ge(out_done, h + 1)
                        if h:
                            act.wait_ge(rms_ready, h)
                        for m in range(TT):
                            if h or m:
                                act.wait_ge(ssq_ready, 2 * h + m)
                            act.activation(squares[:, :], bank[:, 3, m * P:(m + 1) * P], ACT.Square,
                                           accum_out=ssq[:, m:m + 1]).then_inc(ssq_ready, 1)
                    if (b, s) in ((9, 3), (10, 5)):
                        i = b - 9
                        act.wait_ge(slots_done, b * SLOTS)
                        if i:
                            act.wait_ge(four1_done, 1)
                        act.activation(u_hi[:, :, :], acc[i][:, :, :], ACT.Copy).then_inc(u_hi_ready, 1)
                    if (b, s) in ((9, 7), (11, 0)):
                        g = b // 11
                        act.wait_ge(four1_done, g + 1)
                        if g:
                            act.wait_ge(four_ready, 1)
                        for e in range(2):
                            act.activation(by_group(dftT_hi, 0, COSINES)[:, e], made_cosines[:, e], ACT.Copy)
                            ins = act.activation(by_group(dftT_hi, COSINES, 2 * T)[:, e], made_sines[:, e], ACT.Copy)
                        ins.then_inc(dftT_hi_ready, 1)
                    if (b, s) in ((10, 3), (11, 5)):
                        g = b - 10
                        act.wait_ge(four2_done, g + 1)
                        act.activation(halves[:, :, :], bank[:, 0:2, :], ACT.Copy).then_inc(halves_ready, 1)
                    if (b, s) in ((10, 4), (11, 6)):
                        g = b - 10
                        act.wait_ge(four_ready, g + 1)
                        act.activation(mix_hi[:, 8 + 4 * g:12 + 4 * g, :].rearrange("p c t -> p (c t)"),
                                       four_out[:, :, :, :].rearrange("p g c t -> p (g c t)"),
                                       ACT.Copy).then_inc(mix_hi_ready, 1)
                    if (b, s) in ((11, 3), (12, 2)):
                        i = b - 11
                        act.wait_ge(slots_done, b * SLOTS)
                        if i:
                            act.wait_ge(gated_turned, 1)
                        else:
                            act.wait_ge(z_turned, 4)
                        act.activation(tok_z[:, :, :], acc[i][:, :, :], ACT.Sigmoid).then_inc(sig_ready, 1)
                    if (b, s) in ((12, 1), (12, 6)):
                        i = s // 6
                        act.wait_ge(gated_turned, i + 1)
                        for c in range(2):
                            k = 4 * i + 2 * c
                            act.activation(mix_hi[:, k:k + 2, :].rearrange("p c t -> p (c t)"),
                                           bank[:, 2 + c, :], ACT.Copy).then_inc(mix_hi_ready, 1)
            act.wait_ge(mix_ready, 4)
            load_gamma_beta(A["ln1_g"][0], A["ln1_b"][0])
            for n in range((OUT0 + 1) * SLOTS, GLU0 * SLOTS):
                split(n)
            for n in range(GLU0 * SLOTS, (GLU0 + 2) * SLOTS):
                split(n)
                s = n - GLU0 * SLOTS
                if s == 3:
                    for pair in range(4):
                        norm_pair(1, pair)
                if 4 <= s < SLOTS:
                    norm_pair(1, s)
                if s == SLOTS + 3:
                    act.wait_ge(slots_done, (GLU0 + 1) * SLOTS)
                    act.activation(silu[:, :, :], acc[0][:, :, :], ACT.Silu).then_inc(acc_read[0], 1)

            def act_columns(j, c):
                act.activation(act_hi[:, bass.ds(4 * j + 2 * c, 2), :].rearrange("p c t -> p (c t)"),
                               bank[:, c, :], ACT.Copy).then_inc(act_hi_ready, 1)

            with act.Fori(1, GLU) as j:
                for s in range(2 * SLOTS):
                    n = GLU0 * SLOTS + s
                    split_hi(n, s % RING, j * 64 + (16 * 16 + 16 * (n // RING + 1)), j * (2 * SLOTS) + (n - RING + 1))
                    if s in (5, 6):
                        act.wait_ge(act_turned, j)
                        act_columns(j - 1, s - 5)
                    if s == SLOTS + 3:
                        act.wait_ge(slots_done, j * (2 * SLOTS) + (GLU0 + 1) * SLOTS)
                        act.wait_ge(act_turned, j)
                        act.activation(silu[:, :, :], acc[0][:, :, :], ACT.Silu).then_inc(acc_read[0], 1)
            for n in range(DOWN_N0, DOWN_N0 + 4 * DOWN_SLOTS):
                split(n)
                if n == DOWN_N0 + 5:
                    act.wait_ge(act_turned, GLU)
                    act_columns(GLU - 1, 0)
                    act_columns(GLU - 1, 1)
                    act.wait_ge(residual_done, 16)
                    load_gamma_beta(A["ln2_g"][0], A["ln2_b"][0])
            for m in range(TT):
                part = rows[:, m, OWN:D]
                act.wait_ge(shift_ready, m + 1)
                act.activation(part, part, ACT.Identity, bias=shift[:, m:m + 1],
                               scale=rstd[:, m:m + 1]).then_inc(scaled, 1)

        @block.vector
        def _(dve):
            steps = [0]

            def then(ins):
                steps[0] += 1
                ins.then_inc(dve_step, 1)
                dve.wait_ge(dve_step, steps[0])

            def split(n, r=None):
                r = n % RING if r is None else r
                dve.wait_ge(hi_ready, n + 1)
                dve.tensor_tensor(w_lo[r][:, :, :], raw[r][:, :, :], w_hi[r][:, :, :],
                                  ALU.subtract).then_inc(lo_ready, 1)

            def row_stats(q, m):
                return dve.bn_stats(stats[:, m, q, :], rows[:, m, q * NB:(q + 1) * NB])

            def aggregate(m):
                dve.bn_aggr(mean_var[:, m, :], stats[:, m, :, :].rearrange("p q s -> p (q s)")).then_inc(var_ready, 1)

            def normalise(m, first, end):
                part = rows[:, m, first:end]
                return dve.tensor_scalar(part, part, mean_var[:, m, 0:1], rstd[:, m:m + 1],
                                         ALU.subtract, ALU.mult)

            def normalise_quarter(q):
                normalise(0, q * NB, (q + 1) * NB)
                normalise(1, q * NB, (q + 1) * NB).then_inc(normed, 2)

            def normalise_half(i):
                dve.wait_ge(rstd_ready, TT * i + 1)
                if i == 0:
                    normalise(0, 0, 2 * P)
                    dve.wait_ge(rstd_ready, TT * i + 2)
                    normalise(1, 0, 2 * P).then_inc(normed, 1)
                    normalise(0, 2 * P, NB)
                    normalise(1, 2 * P, NB).then_inc(normed, 1)
                    normalise(0, NB, 2 * NB)
                else:
                    normalise(0, 0, NB)
                    normalise(0, NB, 2 * NB)
                    dve.wait_ge(rstd_ready, TT * i + 2)
                    normalise(1, 0, 2 * P).then_inc(normed, 1)
                    normalise(1, 2 * P, NB).then_inc(normed, 1)
                normalise(1, NB, 2 * NB).then_inc(normed, 2)

            def norm_pair(i, s):
                dve.wait_ge(xT_hi_ready, SLOTS * i + s + 1)
                if SLOTS * i + s >= 2:
                    dve.wait_ge(xT_lo_ready, SLOTS * i + s - 1)
                for c in range(2):
                    col = 2 * KC * i + 2 * s + c
                    ins = dve.tensor_scalar(turned[s % 2][:, c, :], bank[:, s % 4, c * T:(c + 1) * T],
                                            vecT[:, col:col + 1], vecT[:, col + KC:col + KC + 1],
                                            ALU.mult, ALU.add)
                    if s == 0:
                        if c == 1:
                            ins.then_inc(turned_ready, 1)
                            dve.wait_ge(turned_ready, SLOTS * i + 1)
                        else:
                            then(ins)
                        dve.tensor_tensor(xT_lo[:, c, :], turned[0][:, c, :], xT_hi[:, c, :], ALU.subtract)\
                           .then_inc((first_lo_ready, xT_lo_ready)[c], 1)
                if s:
                    ins.then_inc(turned_ready, 1)

            def residual(i, m, q):
                cols = slice(q * NB, (q + 1) * NB)
                part = rows[:, m, cols]
                then(dve.scalar_tensor_tensor(part, part, ALPHA, gamma[:, cols], ALU.mult, ALU.mult))
                dve.scalar_tensor_tensor(part, beta[:, cols], ALPHA, part, ALU.mult, ALU.add)\
                   .then_inc(residual_done, 1)

            def add_block(b, q, i):
                a = b % 2
                dve.wait_ge(residual_done, 8 * (i + 1))
                part = rows[:, :, q * NB:(q + 1) * NB]
                ins = dve.tensor_tensor(part, part, acc[a][:, :, :], ALU.add).then_inc(acc_read[a], 1)
                dve.wait_ge(acc_read[a], b // 2 + 1)
                row_stats(q, 0)
                return row_stats(q, 1)

            def add_last_block(b, q, i):
                a = b % 2
                dve.wait_ge(residual_done, 8 * (i + 1))
                for m in range(TT):
                    part = rows[:, m, q * NB:(q + 1) * NB]
                    if m == 0:
                        dve.wait_ge(first_tile_done, i + 1)
                        then(dve.tensor_tensor(part, part, acc[a][:, m, :], ALU.add))
                    else:
                        dve.wait_ge(slots_done, (GLU0 * SLOTS, DOWN_N0 + 4 * DOWN_SLOTS)[i])
                        dve.tensor_tensor(part, part, acc[a][:, m, :], ALU.add).then_inc(acc_read[a], 1)
                        dve.wait_ge(acc_read[a], b // 2 + 1)
                    then(row_stats(q, m))
                    aggregate(m)

            for i in range(2):
                dve.memset(f[i][:, :, :, 0:1], 0.0)
                dve.memset(f[i][:, :, :, T + 1:T + 2], 0.0)
            dve.memset(heads_in[:, :, :], 0.0)
            dve.memset(scoresT[:, :, :, :], 0.0).then_inc(fills_done, 1)

            for q in range(4):
                dve.wait_ge(x_landed[q], 16)
                for m in range(TT):
                    ins = row_stats(q, m)
            then(ins)
            aggregate(0)
            aggregate(1)
            dve.wait_ge(vec_turned, 1)
            dve.tensor_copy(vecT[:, :], bank[:, 3, 0:VEC_ROWS]).then_inc(vec_ready, 1)
            normalise_half(0)
            dve.wait_ge(vec_ready, 1)
            split(0)
            norm_pair(0, 0)
            norm_pair(0, 1)
            split(1)
            normalise_quarter(2)
            norm_pair(0, 2)
            split(2)
            normalise_quarter(3)
            for s in range(3, SLOTS):
                norm_pair(0, s)
                split(s)
            logits = vecT[:, 4 * KC:VEC_ROWS].rearrange("p (d l h) -> p d l h", d=2, l=2)

            def shift_logits():
                then(dve.tensor_tensor(lb_max[:, :, :], logits[:, :, 0, :], logits[:, :, 1, :], ALU.max))
                dve.tensor_tensor(lb_exp[:, :, 0, :], logits[:, :, 0, :], lb_max[:, :, :], ALU.subtract)
                dve.tensor_tensor(lb_exp[:, :, 1, :], logits[:, :, 1, :], lb_max[:, :, :],
                                  ALU.subtract).then_inc(lb_shifted, 1)

            def lower_bounds():
                dve.wait_ge(lb_exped, 1)
                then(dve.tensor_tensor(lb_sum[:, :, :], lb_exp[:, :, 0, :], lb_exp[:, :, 1, :], ALU.add))
                then(dve.reciprocal(lb_sum[:, :, :], lb_sum[:, :, :]))
                then(dve.tensor_tensor(lb[:, :, :], lb_exp[:, :, 0, :], lb_sum[:, :, :], ALU.mult))
                dve.tensor_scalar(one_minus_lb[:, :, :], lb[:, :, :], -1.0, 1.0, ALU.mult, ALU.add)\
                   .then_inc(lb_ready, 1)

            def head_factors(h):
                p, e = h // 2, h % 2
                F = f[p % 2]
                qd = q_dec[h % 2]
                dve.wait_ge(f_ready, 4 * (p + 1))
                dve.wait_ge(qT_ready, p + 1)
                if h:
                    dve.wait_ge(scores_done, h)
                if h >= 2:
                    dve.wait_ge(out_done, h - 1)
                dve.tensor_scalar(k_end[:, :, :], F[:, :, e, 1:T + 1], -1.0, 1.0, ALU.mult, ALU.add)
                dve.tensor_copy(heads_in[:, 0, 0:T:CH], F[:, 0, e, 1:T + 1:CH])
                then(dve.tensor_copy(heads_in[:, 1, CH - 1:T:CH], F[:, 1, e, CH:T + 1:CH]))
                dve.memset(F[:, 0, e, 1:T + 1:CH], 0.0)
                then(dve.memset(F[:, 1, e, CH:T + 1:CH], 0.0))
                dve.tensor_tensor_scan(q_inv[:, 0, :], F[:, 0, e, 1:T + 1], heads_in[:, 0, :], 0.0,
                                       ALU.mult, ALU.add)
                dve.tensor_tensor_scan(q_inv[:, 1, ::-1], F[:, 1, e, T:0:-1], heads_in[:, 1, ::-1], 0.0,
                                       ALU.mult, ALU.add)
                dve.tensor_tensor_scan(qd[:, 0, ::-1], F[:, 0, e, T + 1:1:-1], last_ones[:, ::-1], 0.0,
                                       ALU.mult, ALU.add)
                then(dve.tensor_tensor_scan(qd[:, 1, :], F[:, 1, e, 0:T], first_ones, 0.0,
                                            ALU.mult, ALU.add))

            def head_operands(h):
                p, e = h // 2, h % 2
                qd = q_dec[h % 2]
                dve.tensor_tensor(k_end[:, :, :], k_end[:, :, :], qd[:, :, :], ALU.mult)
                dve.tensor_copy(decay[h % 2][:, 0, :], q_inv[:, 0, CH - 1:T:CH])
                dve.tensor_copy(decay[h % 2][:, 1, :], q_inv[:, 1, 0:T:CH])
                dve.reciprocal(inv_decay[:, 0, :], q_inv[:, 0, CH - 1:T:CH])
                then(dve.reciprocal(inv_decay[:, 1, :], q_inv[:, 1, 0:T:CH]))
                for d in range(2):
                    ins = dve.tensor_tensor(qd[:, d, :], q_inv[:, d, :], qT[p % 2][:, e, :], ALU.mult)
                then(ins)
                for d in range(2):
                    ins = dve.tensor_tensor(q_inv[:, d, :].rearrange("p (c t) -> p c t", t=CH),
                                            qd[:, d, :].rearrange("p (c t) -> p c t", t=CH),
                                            inv_decay[:, d, :].rearrange("p (c a) -> p c a", a=1)
                                            .broadcast_to([P, NCH, CH]), ALU.mult)
                ins.then_inc(head_ready, 1)

            def head_scores(h):
                dve.wait_ge(scores_done, h + 1)
                if h:
                    dve.wait_ge(out_done, h)
                then(dve.copy_predicated(scoresT[:, :, :, :].rearrange("p d m t -> p (d m t)"),
                                         causal.rearrange("p d m t -> p (d m t)"), bank[:, 2, :]))
                dve.tensor_tensor(scores_sum[:, :, :], scoresT[:, 0, :, :], scoresT[:, 1, :, :],
                                  ALU.add).then_inc(scores_ready, 1)

            def head_states(h):
                dve.wait_ge(dstate_done, h + 1)
                if h:
                    dve.wait_ge(out_done, h)
                for d in range(2):
                    then(dve.tensor_copy(state[:, d, 0, :], dstate(d, 0 if d == 0 else 3)))
                    for j in range(1, 3):
                        c = j if d == 0 else 3 - j
                        ins = dve.scalar_tensor_tensor(state[:, d, j, :], state[:, d, j - 1, :],
                                                       decay[h % 2][:, d, c:c + 1], dstate(d, c),
                                                       ALU.mult, ALU.add)
                        if j == 1 or d == 0:
                            then(ins)
                ins.then_inc(states_ready, 1)

            def head_out(h):
                dve.wait_ge(rms_ready, h + 1)
                for m in range(TT):
                    ins = dve.scalar_tensor_tensor(o_heads[:, m, h * P:(h + 1) * P], bank[:, 3, m * P:(m + 1) * P],
                                                   rms[:, m:m + 1], g_norm[:, :], ALU.mult, ALU.mult)
                ins.then_inc(o_ready, 1)

            shift_logits()
            for b in range(1, OUT0 + 1):
                for s in range(SLOTS):
                    split(b * SLOTS + s)
                    if (b, s) == (1, 4):
                        lower_bounds()
                    if b == 1:
                        if s == 0:
                            dve.wait_ge(gb_landed, 32)
                            dve.wait_ge(rows_turned, SLOTS)
                        residual(0, s // 4, s % 4)
                    if b == 2 and s == 0:
                        dve.wait_ge(dft_hi_ready, 1)
                        dve.tensor_tensor(dft_lo[:, :, :], dft_raw[:, :, :], dft_hi[:, :, :],
                                          ALU.subtract).then_inc(dft_ready, 1)
                    if 2 <= b < 10 and b % 2 == 0 and s == 4:
                        p = b // 2 - 1
                        dve.wait_ge(qv_read, 2 * (p + 1))
                        dve.tensor_tensor(tok_q[:, :, :], tok_q[:, :, :], acc[1][:, :, 0:2 * P],
                                          ALU.mult).then_inc(acc_read[1], 1)
                    if 2 <= b < 10 and b % 2 == 0 and s == 7:
                        p = b // 2 - 1
                        dve.wait_ge(q_turned, p + 1)
                        dve.tensor_copy(qT[p % 2][:, :, :].rearrange("p e t -> p (e t)"),
                                        bank[:, 0, :]).then_inc(qT_ready, 1)
                    if 4 <= b < 4 + HEADS and s == 0:
                        head_states(b - 4)
                    if 3 <= b < 3 + HEADS:
                        if s == 1:
                            head_factors(b - 3)
                        if s == 2:
                            head_operands(b - 3)
                        if s == 6:
                            head_scores(b - 3)
                    if 4 <= b < 4 + HEADS and s == 5:
                        head_out(b - 4)
                    if (b, s) in ((9, 4), (10, 5)):
                        i = b - 9
                        dve.wait_ge(u_hi_ready, i + 1)
                        dve.tensor_tensor(u_lo[:, :, :], acc[i][:, :, :], u_hi[:, :, :],
                                          ALU.subtract).then_inc(acc_read[i], 1)
                    if (b, s) in ((9, 7), (11, 0)):
                        g = b // 11
                        dve.wait_ge(dftT_hi_ready, g + 1)
                        if g:
                            dve.wait_ge(mix_hi_ready, 1)
                            dve.wait_ge(mix_ready, 2)
                        for e in range(2):
                            for source, first, end in ((made_cosines, 0, COSINES), (made_sines, COSINES, 2 * T)):
                                ins = dve.tensor_tensor(by_group(dftT_lo, first, end)[:, e], source[:, e],
                                                        by_group(dftT_hi, first, end)[:, e], ALU.subtract)
                        ins.then_inc(dftT_ready, 1)
                    if (b, s) in ((10, 3), (11, 5)):
                        g = b - 10
                        even, odd = by_group(halves, 0, COSINES), by_group(halves, COSINES, 2 * T)
                        dve.wait_ge(halves_ready, g + 1)
                        dve.tensor_copy(four_out[:, :, :, 0:HALF:T // 2], even[:, :, :, 0:HALF:T // 2])
                        for gg in range(2):
                            dve.tensor_tensor(four_out[:, gg, :, HALF:T], even[:, gg, :, SINES:0:-1], odd[:, gg, :, :],
                                              ALU.subtract)
                            ins = dve.tensor_tensor(four_out[:, gg, :, 1:SINES + 1], even[:, gg, :, 1:SINES + 1],
                                                    odd[:, gg, :, ::-1], ALU.add)
                        ins.then_inc(four_ready, 1)
                    if (b, s) in ((10, 4), (11, 6)):
                        g = b - 10
                        dve.wait_ge(four_ready, g + 1)
                        dve.wait_ge(mix_hi_ready, g + 1)
                        dve.tensor_tensor(mix_lo[:, 8 + 4 * g:12 + 4 * g, :].rearrange("p c t -> p (c t)"),
                                          four_out[:, :, :, :].rearrange("p g c t -> p (g c t)"),
                                          mix_hi[:, 8 + 4 * g:12 + 4 * g, :].rearrange("p c t -> p (c t)"),
                                          ALU.subtract).then_inc(mix_ready, 2)
                    if (b, s) in ((11, 4), (12, 3)):
                        i = b - 11
                        dve.wait_ge(sig_ready, i + 1)
                        dve.tensor_tensor(tok_z[:, :, :], tok_z[:, :, :], acc[i][:, :, :],
                                          ALU.mult).then_inc(acc_read[i], 1)
                        dve.wait_ge(acc_read[i], 6)
                        dve.wait_ge(o_ready, 4 * (i + 1))
                    if (b, s) in ((11, 5), (12, 4)):
                        i = b - 11
                        dve.tensor_tensor(tok_z[:, :, :], tok_z[:, :, :], o_heads[:, :, i * NB:(i + 1) * NB],
                                          ALU.mult).then_inc(gated, 1)
                    if (b, s) in ((12, 1), (12, 6)):
                        i = s // 6
                        for c in range(2):
                            k = 4 * i + 2 * c
                            dve.wait_ge(mix_hi_ready, 3 + 2 * i + c)
                            dve.tensor_tensor(mix_lo[:, k:k + 2, :].rearrange("p c t -> p (c t)"),
                                              bank[:, 2 + c, :],
                                              mix_hi[:, k:k + 2, :].rearrange("p c t -> p (c t)"),
                                              ALU.subtract).then_inc(mix_ready, 1)
            for n in range((OUT0 + 1) * SLOTS, GLU0 * SLOTS):
                split(n)
                if n % SLOTS == 3:
                    b = n // SLOTS - 1
                    dve.wait_ge(slots_done, (b + 1) * SLOTS)
                    add_block(b, b - OUT0, 0)
            for s in range(2):
                split(GLU0 * SLOTS + s)
            add_last_block(GLU0 - 1, 3, 0)
            normalise_half(1)
            split(GLU0 * SLOTS + 2)
            norm_pair(1, 0)
            norm_pair(1, 1)
            normalise_quarter(2)
            split(GLU0 * SLOTS + 3)
            norm_pair(1, 2)
            normalise_quarter(3)
            norm_pair(1, 3)
            for s in range(4, SLOTS):
                split(GLU0 * SLOTS + s)
                norm_pair(1, s)
            dve.wait_ge(gb_landed, 64)
            dve.wait_ge(rows_turned, 2 * SLOTS)
            for s in range(SLOTS):
                split((GLU0 + 1) * SLOTS + s)
                residual(1, s // 4, s % 4)

            def glu(j):
                dve.wait_ge(acc_read[0], j + (GLU0 // 2 + 1))
                dve.wait_ge(slots_done, j * (2 * SLOTS) + (GLU0 + 2) * SLOTS)
                dve.tensor_tensor(silu[:, :, :], silu[:, :, :], acc[1][:, :, :], ALU.mult).then_inc(acc_read[1], 1)

            def act_columns(j, c):
                cols = act_hi[:, bass.ds(4 * j + 2 * c, 2), :].rearrange("p c t -> p (c t)")
                low = act_lo[:, bass.ds(4 * j + 2 * c, 2), :].rearrange("p c t -> p (c t)")
                dve.wait_ge(act_hi_ready, 2 * j + c + 1)
                dve.tensor_tensor(low, bank[:, c, :], cols, ALU.subtract).then_inc(act_ready, 1)

            with dve.Fori(1, GLU) as j:
                for s in range(2 * SLOTS):
                    split(j * (2 * SLOTS) + (GLU0 * SLOTS + s), s % RING)
                    if s == 3:
                        glu(j - 1)
                    if s in (5, 6):
                        act_columns(j - 1, s - 5)
            for n in range(4 * DOWN_SLOTS):
                split(DOWN_N0 + n)
                if n == 2:
                    glu(GLU - 1)
                if n in (5, 6):
                    act_columns(GLU - 1, n - 5)
                if n > DOWN_SLOTS and n % DOWN_SLOTS == 3:
                    b = n // DOWN_SLOTS - 1
                    dve.wait_ge(slots_done, DOWN_N0 + (b + 1) * DOWN_SLOTS)
                    add_block(DOWN0 + b, b, 1)
            add_last_block(DOWN0 + 3, 3, 1)
            dve.wait_ge(gb_landed, 96)
            pieces = [slice(q * NB, min((q + 1) * NB, OWN)) for q in range(3)]

            def make_shift(m):
                dve.wait_ge(rstd_ready, 2 * TT + m + 1)
                dve.scalar_tensor_tensor(shift[:, m:m + 1], mean_var[:, m, 0:1], -1.0, rstd[:, m:m + 1],
                                         ALU.mult, ALU.mult).then_inc(shift_ready, 1)

            make_shift(0)
            for m in range(TT):
                for cols in pieces:
                    part = rows[:, m, cols]
                    ins = dve.scalar_tensor_tensor(part, part, mean_var[:, m, 0:1], gamma[:, cols],
                                                   ALU.subtract, ALU.mult)
                then(ins)
                if m == 0:
                    make_shift(1)
                for cols in pieces:
                    part = rows[:, m, cols]
                    dve.scalar_tensor_tensor(part, part, rstd[:, m:m + 1], beta[:, cols],
                                             ALU.mult, ALU.add).then_inc(out_ready, 1)

        @block.tensor
        def _(pe):
            def products(a, r, c, m, k, left_hi, left_lo, first, last):
                out = acc[a][:, m, :]
                hi, lo = left_hi[:, k, m * P:(m + 1) * P], left_lo[:, k, m * P:(m + 1) * P]
                pe.matmul(out, hi, w_hi[r][:, c, :], start=first, stop=False)
                pe.matmul(out, hi, w_lo[r][:, c, :], start=False, stop=False)
                return pe.matmul(out, lo, w_hi[r][:, c, :], start=False, stop=last)

            def slot(n, r, a, left_hi, left_lo, k0, first, last, first_chunk=None):
                pe.wait_ge(lo_ready, n + 1)
                for c in range(2):
                    if c == 1 and first_chunk is not None:
                        pe.wait_ge(xT_lo_ready, first_chunk)
                    for m in range(TT):
                        ins = products(a, r, c, m, k0 + c, left_hi, left_lo, first and c == 0, last and c == 1)
                ins.then_inc(slots_done, 1)

            def last_slot(n, r, a, left_hi, left_lo, k0):
                pe.wait_ge(lo_ready, n + 1)
                for m in range(TT):
                    for c in range(2):
                        ins = products(a, r, c, m, k0 + c, left_hi, left_lo, False, c == 1)
                    ins.then_inc((first_tile_done, slots_done)[m], 1)

            def turn_rows(i, s):
                if i == 0 and s == 3:
                    pe.wait_ge(vec_ready, 1)
                pe.wait_ge(normed, SLOTS * i + s + 1)
                if s >= 4:
                    pe.wait_ge(turned_ready, SLOTS * i + s - 3)
                for c in range(2):
                    k = 2 * s + c
                    for m in range(TT):
                        ins = pe.transpose(bank[:, s % 4, c * T + m * P:c * T + (m + 1) * P],
                                           rows[:, m, k * P:(k + 1) * P], ident[:, :])
                ins.then_inc(rows_turned, 1)

            def turn(b, cols, source, done):
                for t in range(2):
                    for m in range(TT):
                        ins = pe.transpose(bank[:, b, t * T + m * P:t * T + (m + 1) * P],
                                           source[:, m, cols + t * P:cols + (t + 1) * P], ident[:, :])
                if done is not None:
                    ins.then_inc(done, 1)

            def head_scores(h):
                pe.wait_ge(head_ready, h + 1)
                if h:
                    pe.wait_ge(o_ready, h)
                for d in range(2):
                    for m in range(TT):
                        ins = pe.transpose(bank[:, 3, (2 * d + m) * P:(2 * d + m + 1) * P],
                                           k_end[:, d, m * P:(m + 1) * P], ident[:, :])
                ins.then_inc(k_turned, 1)
                for d in range(2):
                    for m in range(TT):
                        ins = pe.matmul(bank[:, 2, (2 * d + m) * P:(2 * d + m + 1) * P],
                                        k_end[:, d, m * P:(m + 1) * P], q_inv[:, d, m * P:(m + 1) * P],
                                        start=True, stop=True)
                ins.then_inc(scores_done, 1)

            def head_dstates(h):
                p, e = h // 2, h % 2
                pe.wait_ge(k_rows_ready, h + 1)
                pe.wait_ge(scores_ready, h + 1)
                for d, c in ((0, 0), (0, 1), (0, 2), (1, 3), (1, 2), (1, 1)):
                    part = slice(CH * (c % 2), CH * (c % 2) + CH)
                    ins = pe.matmul(dstate(d, c), k_rows[part, d, c // 2, :],
                                    v[p % 2][part, c // 2, e * P:(e + 1) * P], start=True, stop=True)
                ins.then_inc(dstate_done, 1)

            def head_out(h):
                p, e = h // 2, h % 2
                pe.wait_ge(states_ready, h + 1)
                for m in range(TT):
                    vals = v[p % 2][:, m, e * P:(e + 1) * P]
                    pe.matmul(bank[:, 3, m * P:(m + 1) * P], scores_sum[:, m, :], vals, start=True, stop=False,
                              skip_group_check=True)
                    for c, d in ((1, 0), (0, 1), (1, 1)) if m == 0 else ((2, 1), (3, 0), (2, 0)):
                        out = bank[CH * (c % 2):CH * (c % 2) + CH, 3, m * P:(m + 1) * P]
                        j = c - 1 if d == 0 else 2 - c
                        ins = pe.matmul(out, q_dec[h % 2][:, d, c * CH:(c + 1) * CH], state[:, d, j, :],
                                        start=False, stop=True, skip_group_check=True)
                ins.then_inc(out_done, 1)

            def fourier_tokens(g):
                cols = slice(HALF, HALF + T)
                for e in range(2):
                    for ch in range(2):
                        out = bank[:, e, ch * T:(ch + 1) * T]
                        first = e * T + ch * P
                        for tc in range(TT):
                            hi, lo = u_hi[:, tc, first:first + P], u_lo[:, tc, first:first + P]
                            pe.matmul(out, hi, dft_hi[:, tc, cols], start=(tc == 0), stop=False)
                            pe.matmul(out, hi, dft_lo[:, tc, cols], start=False, stop=False)
                            ins = pe.matmul(out, lo, dft_hi[:, tc, cols], start=False, stop=(tc == 1))
                ins.then_inc(four1_done, 1)

            def fourier_channels(g):
                pe.wait_ge(dftT_ready, g + 1)
                for ct in range(2):
                    for part, table in ((slice(0, COSINES), T), (slice(COSINES, 2 * T), 0)):
                        out = bank[:, ct, part]
                        cols = slice(table + ct * P, table + (ct + 1) * P)
                        for ch in range(2):
                            hi, lo = dftT_hi[:, ch, part], dftT_lo[:, ch, part]
                            pe.matmul(out, dft_hi[:, ch, cols], hi, start=(ch == 0), stop=False)
                            pe.matmul(out, dft_hi[:, ch, cols], lo, start=False, stop=False)
                            ins = pe.matmul(out, dft_lo[:, ch, cols], hi, start=False, stop=(ch == 1))
                ins.then_inc(four2_done, 1)

            def keep_warm(count, left, right):
                for _ in range(count):
                    pe.matmul(bank[:, 3, :], left, right, start=True, stop=True)

            pe.wait_ge(fills_done, 1)
            pe.wait_ge(x_landed[1], 16)
            zeros = scoresT[:, :, :, :].rearrange("p d m t -> p (d m t)").bitcast(BF16)
            keep_warm(12, zeros[:, 0:P], zeros[:, 0:NB])
            pe.wait_ge(vec_landed, 16 * 6)
            pe.wait_ge(ident_landed, 16)
            pe.transpose(bank[:, 3, 0:VEC_ROWS], vec_rows[:, :], ident[0:VEC_ROWS, 0:VEC_ROWS]).then_inc(vec_turned, 1)

            for s in range(4):
                turn_rows(0, s)
            for b in range(OUT0):
                if b >= 2:
                    pe.wait_ge(acc_read[b % 2], b // 2)
                for s in range(SLOTS):
                    if b == 0 and s == 0:
                        pe.wait_ge(first_lo_ready, 1)
                    elif b == 0:
                        pe.wait_ge(xT_lo_ready, s + 1)
                    slot(b * SLOTS + s, s % RING, b % 2, xT_hi, xT_lo, 2 * s, s == 0, s == SLOTS - 1,
                         1 if b == 0 and s == 0 else None)
                    if b == 0 and s < 4:
                        turn_rows(0, s + 4)
                    if b < 9 and b % 2 == 1 and s == 3:
                        p = b // 2
                        pe.wait_ge(acc_read[0], p + 1)
                        if p:
                            pe.wait_ge(qT_ready, p)
                        else:
                            pe.wait_ge(xT_lo_ready, SLOTS)
                        turn(0, 0, tok_z, None)
                        turn(1, 2 * P, tok_z, z_turned)
                    if 2 <= b < 10 and b % 2 == 0 and s == 3:
                        p = b // 2 - 1
                        pe.wait_ge(acc_read[1], p + 1)
                        pe.wait_ge(f_ready, 4 * (p + 1))
                        turn(0, 0, tok_q, q_turned)
                    if 4 <= b < 4 + HEADS and s == 1:
                        head_out(b - 4)
                    if 3 <= b < 3 + HEADS:
                        if s == 4:
                            head_scores(b - 3)
                        if s == 6:
                            head_dstates(b - 3)
                    if (b, s) == (9, 4):
                        pe.wait_ge(acc_read[0], 5)
                        pe.wait_ge(dft_ready, 1)
                        fourier_tokens(0)
                    if (b, s) == (10, 0):
                        fourier_channels(0)
                    if (b, s) == (10, 5):
                        pe.wait_ge(acc_read[1], 5)
                        pe.wait_ge(halves_ready, 1)
                        fourier_tokens(1)
                    if (b, s) == (11, 1):
                        fourier_channels(1)
                    if (b, s) == (11, 6):
                        pe.wait_ge(gated, 1)
                        pe.wait_ge(o_ready, HEADS)
                        turn(2, 0, tok_z, None)
                        turn(3, 2 * P, tok_z, gated_turned)

            pe.wait_ge(acc_read[0], 6)
            for s in range(SLOTS):
                pe.wait_ge(mix_ready, s + 1)
                slot(OUT0 * SLOTS + s, s % RING, 0, mix_hi, mix_lo, MIX_ORDER[s], s == 0, s == SLOTS - 1)
                if s == 4:
                    pe.wait_ge(gated, 2)
                    pe.wait_ge(mix_ready, 6)
                    turn(2, 0, tok_z, None)
                    turn(3, 2 * P, tok_z, gated_turned)
            for b in range(OUT0 + 1, GLU0):
                pe.wait_ge(acc_read[b % 2], b // 2)
                for s in range(SLOTS if b < GLU0 - 1 else SLOTS - 1):
                    slot(b * SLOTS + s, s % RING, b % 2, mix_hi, mix_lo, MIX_ORDER[s], s == 0, s == SLOTS - 1)
            last_slot(GLU0 * SLOTS - 1, RING - 1, 1, mix_hi, mix_lo, MIX_ORDER[-1])

            keep_warm(14, mix_hi[:, 0, 0:P], mix_hi[:, 0:2, :].rearrange("p c t -> p (c t)"))
            for s in range(4):
                turn_rows(1, s)
            for b in (GLU0, GLU0 + 1):
                pe.wait_ge(acc_read[b % 2], b // 2)
                for s in range(SLOTS):
                    if b == GLU0 and s == 0:
                        pe.wait_ge(first_lo_ready, 2)
                    elif b == GLU0:
                        pe.wait_ge(xT_lo_ready, SLOTS + s + 1)
                    slot(b * SLOTS + s, s % RING, b % 2, xT_hi, xT_lo, 2 * s, s == 0, s == SLOTS - 1,
                         SLOTS + 1 if b == GLU0 and s == 0 else None)
                    if b == GLU0 and s < 4:
                        turn_rows(1, s + 4)

            def turn_act(j):
                pe.wait_ge(acc_read[1], j + (GLU0 // 2 + 1))
                turn(0, 0, silu, None)
                turn(1, 2 * P, silu, act_turned)

            with pe.Fori(1, GLU) as j:
                for a in range(2):
                    pe.wait_ge(acc_read[a], j + GLU0 // 2)
                    for s in range(SLOTS):
                        slot(j * (2 * SLOTS) + ((GLU0 + a) * SLOTS + s), s % RING, a, xT_hi, xT_lo, 2 * s,
                             s == 0, s == SLOTS - 1)
                        if a == 0 and s == 3:
                            turn_act(j - 1)
            for b in range(4):
                pe.wait_ge(acc_read[b % 2], (DOWN0 + b) // 2)
                for s in range(DOWN_SLOTS if b < 3 else DOWN_SLOTS - 1):
                    n = b * DOWN_SLOTS + s
                    if (b, s) == (0, 1):
                        turn_act(GLU - 1)
                    if (b, s) == (0, DOWN_SLOTS - 2):
                        pe.wait_ge(act_ready, 2 * GLU)
                    slot(DOWN_N0 + n, n % RING, b % 2, act_hi, act_lo, 2 * s, s == 0, s == DOWN_SLOTS - 1)
            last_slot(DOWN_N0 + 4 * DOWN_SLOTS - 1, RING - 1, 1, act_hi, act_lo, FC - 2)


def kernel(**inputs):
    import numpy as np
    import concourse.bacc as bacc
    from concourse.bass_utils import run_bass_kernel_spmd

    t = np.arange(T)
    first = np.tile((t % CH == 0).astype(np.float32), (P, 1))
    last = np.tile((t % CH == CH - 1).astype(np.float32), (P, 1))
    s_, t_ = np.arange(P)[:, None], np.arange(P)[None, :]
    same = s_ // CH == t_ // CH
    masks = [(same & (s_ <= t_)).astype(np.float32), (same & (s_ >= t_)).astype(np.float32)]
    consts = np.concatenate([np.eye(P, dtype=np.float32), first, last] + [m for m in masks for _ in range(TT)], axis=1)
    angle = 2.0 * np.pi * (np.outer(t, t) % T) / T
    dft = np.concatenate([np.sin(angle), np.cos(angle)], axis=1) / 16.0

    nc = bacc.Bacc("TRN2", target_bir_lowering=False, num_devices=1)
    arrays = {name: np.ascontiguousarray(a) for name, a in inputs.items()}
    arrays["consts"] = np.ascontiguousarray(consts, dtype=np.float32)
    arrays["dft"] = np.ascontiguousarray(dft, dtype=np.float32)
    A, feeds = {}, {}
    for name, a in arrays.items():
        A[name] = nc.dram_tensor(f"in_{name}", a.shape, mybir.dt.from_np(a.dtype), kind="ExternalInput").ap()
        feeds[f"in_{name}"] = a
    A["out"] = nc.dram_tensor("out_x", (1, T, D), F32, kind="ExternalOutput").ap()
    build(nc, A)
    r = run_bass_kernel_spmd(nc, [feeds], core_ids=[0])
    return r.results[0]["out_x"]
```
